# Optimizing a Trainium2 kernel written in Bass

```python
import math
import jax, jax.numpy as jnp
from jax import lax
import numpy as np

D_MODEL = 1024
BATCH = 1
SEQ = 512
DEPTH = 1

HEAD_DIM = 64
BRANCH_W = D_MODEL // 4
N_BRANCH = 4
N_HEADS = BRANCH_W // HEAD_DIM
SC_K = 3
SB_BLOCK = 128
SSM_GROUPS = 2
SSM_STATE = 64
SSM_CONV_K = 4
SSM_CHUNK = 256
SSM_CONV_DIM = BRANCH_W + 2 * SSM_GROUPS * SSM_STATE
MOBA_BLOCK = 256
MOBA_TOPK = 3
MOBA_QCHUNK = 128
SEQ_MULTIPLE = 256
FFN_HIDDEN = ((8 * D_MODEL + 3 * 256 - 1) // (3 * 256)) * 256
RMS_EPS = 1e-6

W_A_IN = 3 * BRANCH_W
W_B_IN = 3 * BRANCH_W
W_C_IN = BRANCH_W + SSM_CONV_DIM + N_HEADS
W_D_IN = 3 * BRANCH_W
W_G_IN = N_BRANCH * D_MODEL
IN_SPLITS = [W_A_IN, W_A_IN + W_B_IN, W_A_IN + W_B_IN + W_C_IN,
             W_A_IN + W_B_IN + W_C_IN + W_D_IN]
N_IN = W_A_IN + W_B_IN + W_C_IN + W_D_IN + W_G_IN


def rmsnorm(x, g):
    xf = x.astype(jnp.float32)
    y = xf * lax.rsqrt(jnp.mean(xf * xf, axis=-1, keepdims=True) + RMS_EPS)
    return (y * g.astype(jnp.float32)).astype(x.dtype)

def causal_depthwise_conv(x, w):
    k = w.shape[0]
    return lax.conv_general_dilated(
        x, w[:, None, :].astype(x.dtype), window_strides=(1,), padding=[(k - 1, 0)],
        dimension_numbers=("NWC", "WIO", "NWC"), feature_group_count=x.shape[-1])

def short_conv_mixer(u, conv_w):
    xa, b_gate, c_gate = jnp.split(u, 3, axis=-1)
    return b_gate * causal_depthwise_conv(c_gate * xa, conv_w)

def stick_breaking_attention(q, k, v):
    bsz, seq, nh, dh = q.shape
    nqb = seq // SB_BLOCK
    f32 = jnp.float32
    qs = q * (dh ** -0.5)
    within_mat = jnp.tril(jnp.ones((SB_BLOCK, SB_BLOCK), f32), -1)
    outs = []
    for c in range(nqb):
        nkb = c + 1
        kc = nkb * SB_BLOCK
        qi = qs[:, c * SB_BLOCK:(c + 1) * SB_BLOCK]
        z = jnp.einsum("bqhd,bkhd->bhqk", qi, k[:, :kc], preferred_element_type=f32)
        q_pos = c * SB_BLOCK + jnp.arange(SB_BLOCK)
        past = jnp.arange(kc)[None, :] < q_pos[:, None]
        z = jnp.where(past, z, -jnp.inf)
        sp = jax.nn.softplus(z)
        lk = sp.reshape(bsz, nh, SB_BLOCK, nkb, SB_BLOCK)
        within = jnp.einsum("bhqnj,js->bhqns", lk, within_mat)
        after_mat = jnp.tril(jnp.ones((nkb, nkb), f32), -1)
        after = jnp.einsum("bhqm,mn->bhqn", jnp.sum(lk, axis=-1), after_mat)
        between = (within + after[..., None]).reshape(bsz, nh, SB_BLOCK, kc)
        w = jnp.exp(z - sp - between)
        outs.append(jnp.einsum("bhqk,bkhd->bqhd", w.astype(v.dtype), v[:, :kc]))
    return jnp.concatenate(outs, axis=1).reshape(bsz, seq, nh * dh)

def ssd_chunked(x, a, b_in, c_in):
    bsz, seq, nh, hp = x.shape
    ng, ns = b_in.shape[2], b_in.shape[3]
    ne = nh // ng
    t = SSM_CHUNK
    nc = seq // t
    f32 = jnp.float32
    x = x.astype(f32).reshape(bsz, nc, t, ng, ne, hp)
    a = a.astype(f32).reshape(bsz, nc, t, ng, ne)
    bc = b_in.astype(f32).reshape(bsz, nc, t, ng, ns)
    cc = c_in.astype(f32).reshape(bsz, nc, t, ng, ns)
    a_cs = jnp.cumsum(a, axis=2)
    causal = jnp.tril(jnp.ones((t, t), dtype=bool))[:, :, None, None]
    seg = a_cs[:, :, :, None] - a_cs[:, :, None, :]
    decay = jnp.exp(jnp.where(causal, seg, -jnp.inf))
    cb = jnp.einsum("bclgn,bcsgn->bclsg", cc, bc)
    y_diag = jnp.einsum("bclsge,bcsgep->bclgep", cb[..., None] * decay, x)
    decay_to_end = jnp.exp(a_cs[:, :, -1:] - a_cs)
    chunk_states = jnp.einsum("bclgn,bclge,bclgep->bcgepn", bc, decay_to_end, x)
    chunk_decay = jnp.exp(a_cs[:, :, -1])

    def step(h, inp):
        s_c, d_c = inp
        return h * d_c[..., None, None] + s_c, h

    h0 = jnp.zeros((bsz, ng, ne, hp, ns), f32)
    _, h_enter = lax.scan(step, h0, (jnp.moveaxis(chunk_states, 1, 0),
                                     jnp.moveaxis(chunk_decay, 1, 0)))
    h_enter = jnp.moveaxis(h_enter, 0, 1)
    y_off = jnp.einsum("bclgn,bcgepn,bclge->bclgep", cc, h_enter, jnp.exp(a_cs))
    return (y_diag + y_off).reshape(bsz, seq, nh, hp)

def mamba2_mixer(u, conv_w, conv_b, dt_bias, a_log, d_skip, norm_g):
    bsz, seq, _ = u.shape
    z, xbc, dt = jnp.split(u, [BRANCH_W, BRANCH_W + SSM_CONV_DIM], axis=-1)
    xbc = jax.nn.silu(causal_depthwise_conv(xbc, conv_w) + conv_b)
    xs, b_in, c_in = jnp.split(xbc, [BRANCH_W, BRANCH_W + SSM_GROUPS * SSM_STATE], axis=-1)
    dt = jax.nn.softplus(dt.astype(jnp.float32) + dt_bias.astype(jnp.float32))
    a = -jnp.exp(a_log.astype(jnp.float32))
    xh = xs.reshape(bsz, seq, N_HEADS, HEAD_DIM)
    y = ssd_chunked(xh.astype(jnp.float32) * dt[..., None], dt * a,
                    b_in.reshape(bsz, seq, SSM_GROUPS, SSM_STATE),
                    c_in.reshape(bsz, seq, SSM_GROUPS, SSM_STATE))
    y = y.astype(u.dtype) + xh * d_skip[:, None]
    gsz = BRANCH_W // SSM_GROUPS
    gated = y.reshape(bsz, seq, SSM_GROUPS, gsz) * jax.nn.silu(z.reshape(bsz, seq, SSM_GROUPS, gsz))
    return rmsnorm(gated, norm_g.reshape(SSM_GROUPS, gsz)).reshape(bsz, seq, BRANCH_W)

def moba_head(q, k, v):
    seq, dh = q.shape
    nb = seq // MOBA_BLOCK
    ke = max(1, min(MOBA_TOPK, nb - 1))
    cq = MOBA_QCHUNK
    n_pairs = seq * ke
    n_chunks = -(-(n_pairs + (nb + 1) * (cq - 1)) // cq)
    scale = dh ** -0.5
    f32 = jnp.float32
    kblk = k.reshape(nb, MOBA_BLOCK, dh)
    vblk = v.reshape(nb, MOBA_BLOCK, dh)
    k_mean = jnp.mean(kblk.astype(f32), axis=1)
    gate = q.astype(f32) @ k_mean.T
    own = jnp.arange(seq) // MOBA_BLOCK
    gate = jnp.where(jnp.arange(nb)[None, :] < own[:, None], gate, -jnp.inf)
    _, sel = lax.top_k(gate, ke)
    valid = jnp.arange(ke)[None, :] < own[:, None]
    grp = jnp.where(valid, sel, nb).reshape(n_pairs)
    cnt = jnp.zeros((nb + 1,), jnp.int32).at[grp].add(1)
    padded = (cnt + cq - 1) // cq * cq
    pad_end = jnp.cumsum(padded)
    pad_start = pad_end - padded
    order = jnp.argsort(grp, stable=True)
    g_sorted = grp[order]
    rank = jnp.arange(n_pairs, dtype=jnp.int32) - (jnp.cumsum(cnt) - cnt)[g_sorted]
    dest = jnp.zeros((n_pairs,), jnp.int32).at[order].set(pad_start[g_sorted] + rank)
    slot_pair = jnp.full((n_chunks * cq,), -1, jnp.int32).at[dest].set(
        jnp.arange(n_pairs, dtype=jnp.int32)).reshape(n_chunks, cq)
    chunk_grp = jnp.searchsorted(pad_end, jnp.arange(n_chunks, dtype=jnp.int32) * cq, side="right")
    slot_ok = (slot_pair >= 0) & (chunk_grp < nb)[:, None]
    blk = jnp.minimum(chunk_grp, nb - 1)
    q_c = q[jnp.maximum(slot_pair, 0) // ke]
    k_c = kblk[blk]
    v_c = vblk[blk]
    s = jnp.einsum("cqd,ckd->cqk", q_c, k_c, preferred_element_type=f32) * scale
    s = jnp.where(slot_ok[..., None], s, -jnp.inf)
    m = jnp.where(slot_ok, jnp.max(s, axis=-1), 0.0)
    p = jnp.exp(s - m[..., None])
    l = jnp.sum(p, axis=-1)
    o = jnp.einsum("cqk,ckd->cqd", p.astype(v.dtype), v_c, preferred_element_type=f32)
    m_p = m.reshape(-1)[dest].reshape(seq, ke)
    l_p = l.reshape(-1)[dest].reshape(seq, ke)
    o_p = o.reshape(-1, dh)[dest].reshape(seq, ke, dh)
    s_own = jnp.einsum("nqd,nkd->nqk", q.reshape(nb, MOBA_BLOCK, dh), kblk,
                       preferred_element_type=f32) * scale
    s_own = jnp.where(jnp.tril(jnp.ones((MOBA_BLOCK, MOBA_BLOCK), dtype=bool)), s_own, -jnp.inf)
    m_own = jnp.max(s_own, axis=-1)
    p_own = jnp.exp(s_own - m_own[..., None])
    l_own = jnp.sum(p_own, axis=-1).reshape(seq)
    o_own = jnp.einsum("nqk,nkd->nqd", p_own.astype(v.dtype), vblk,
                       preferred_element_type=f32).reshape(seq, dh)
    m_own = m_own.reshape(seq)
    m_all = jnp.maximum(m_own, jnp.max(jnp.where(valid, m_p, -jnp.inf), axis=-1))
    w_p = jnp.where(valid, jnp.exp(m_p - m_all[:, None]), 0.0)
    w_own = jnp.exp(m_own - m_all)
    num = w_own[:, None] * o_own + jnp.einsum("sr,srd->sd", w_p, o_p)
    den = w_own * l_own + jnp.sum(w_p * l_p, axis=-1)
    return (num / den[:, None]).astype(q.dtype)

def moba_attention(q, k, v):
    bsz, seq, nh, dh = q.shape
    qt, kt, vt = [jnp.moveaxis(t, 2, 1) for t in (q, k, v)]
    out = lax.map(lambda a: jax.vmap(moba_head)(*a), (qt, kt, vt))
    return jnp.moveaxis(out, 1, 2).reshape(bsz, seq, nh * dh)

def hybrid_layer(x, norm1_g, w_in, conv_a_w, ssm_conv_w, ssm_conv_b, ssm_dt_bias,
                 ssm_a_log, ssm_d, ssm_norm_g, w_branch, w_o, norm2_g, w_gate_up, w_down):
    bsz, seq, _ = x.shape
    h = rmsnorm(x, norm1_g)
    u = h @ w_in
    u_a, u_b, u_c, u_d, u_g = jnp.split(u, IN_SPLITS, axis=-1)
    y_a = short_conv_mixer(u_a, conv_a_w)
    q_b, k_b, v_b = [t.reshape(bsz, seq, N_HEADS, HEAD_DIM) for t in jnp.split(u_b, 3, axis=-1)]
    y_b = stick_breaking_attention(q_b, k_b, v_b)
    y_c = mamba2_mixer(u_c, ssm_conv_w, ssm_conv_b, ssm_dt_bias, ssm_a_log, ssm_d, ssm_norm_g)
    q_d, k_d, v_d = [t.reshape(bsz, seq, N_HEADS, HEAD_DIM) for t in jnp.split(u_d, 3, axis=-1)]
    y_d = moba_attention(q_d, k_d, v_d)
    gates = jax.nn.sigmoid(u_g.reshape(bsz, seq, N_BRANCH, D_MODEL))
    branches = [y_a, y_b, y_c, y_d]
    merged = gates[:, :, 0] * (branches[0] @ w_branch[0])
    for i in range(1, N_BRANCH):
        merged = merged + gates[:, :, i] * (branches[i] @ w_branch[i])
    x = x + merged @ w_o
    h2 = rmsnorm(x, norm2_g)
    g_ff, up_ff = jnp.split(h2 @ w_gate_up, 2, axis=-1)
    return x + (jax.nn.silu(g_ff) * up_ff) @ w_down

def first_inputs(seed: int = 0) -> dict:
    key = jax.random.key(seed)
    ks = jax.random.split(key, 17)
    f32 = jnp.float32

    def nrm(k, shape, scale):
        return jax.random.normal(k, shape, f32) * scale

    dt0 = jnp.exp(jax.random.uniform(ks[6], (DEPTH, N_HEADS), f32, math.log(1e-3), math.log(1e-1)))
    return {
        "x": nrm(ks[0], (BATCH, SEQ, D_MODEL), 1.0),
        "norm1_g": 1.0 + nrm(ks[1], (DEPTH, D_MODEL), 0.02),
        "w_in": nrm(ks[2], (DEPTH, D_MODEL, N_IN), D_MODEL ** -0.5),
        "conv_a_w": nrm(ks[3], (DEPTH, SC_K, BRANCH_W), SC_K ** -0.5),
        "ssm_conv_w": nrm(ks[4], (DEPTH, SSM_CONV_K, SSM_CONV_DIM), SSM_CONV_K ** -0.5),
        "ssm_conv_b": nrm(ks[5], (DEPTH, SSM_CONV_DIM), 0.02),
        "ssm_dt_bias": dt0 + jnp.log(-jnp.expm1(-dt0)),
        "ssm_a_log": jnp.log(jax.random.uniform(ks[7], (DEPTH, N_HEADS), f32, 1.0, 16.0)),
        "ssm_d": 1.0 + nrm(ks[8], (DEPTH, N_HEADS), 0.1),
        "ssm_norm_g": 1.0 + nrm(ks[9], (DEPTH, BRANCH_W), 0.02),
        "w_branch": nrm(ks[10], (DEPTH, N_BRANCH, BRANCH_W, D_MODEL), BRANCH_W ** -0.5),
        "w_o": nrm(ks[11], (DEPTH, D_MODEL, D_MODEL), D_MODEL ** -0.5),
        "norm2_g": 1.0 + nrm(ks[12], (DEPTH, D_MODEL), 0.02),
        "w_gate_up": nrm(ks[13], (DEPTH, D_MODEL, 2 * FFN_HIDDEN), D_MODEL ** -0.5),
        "w_down": nrm(ks[14], (DEPTH, FFN_HIDDEN, D_MODEL), FFN_HIDDEN ** -0.5),
        "final_g": 1.0 + nrm(ks[15], (D_MODEL,), 0.02),
    }

def first_block(x, norm1_g, w_in, conv_a_w, ssm_conv_w, ssm_conv_b, ssm_dt_bias, ssm_a_log,
              ssm_d, ssm_norm_g, w_branch, w_o, norm2_g, w_gate_up, w_down, final_g):
    seq = x.shape[1]
    seq_pad = -(-seq // SEQ_MULTIPLE) * SEQ_MULTIPLE
    h = jnp.pad(x, ((0, 0), (0, seq_pad - seq), (0, 0)))
    for l in range(DEPTH):
        h = hybrid_layer(h, norm1_g[l], w_in[l], conv_a_w[l], ssm_conv_w[l], ssm_conv_b[l],
                         ssm_dt_bias[l], ssm_a_log[l], ssm_d[l], ssm_norm_g[l], w_branch[l],
                         w_o[l], norm2_g[l], w_gate_up[l], w_down[l])
    return rmsnorm(h, final_g)[:, :seq]


CHUNK = 64
EPS = 1e-6

ATT_HEADS = 16
ATT_KV_HEADS = 2
ATT_GROUP = ATT_HEADS // ATT_KV_HEADS
ATT_WIDTH = ATT_HEADS * HEAD_DIM
KV_WIDTH = ATT_KV_HEADS * HEAD_DIM
WINDOW = 128
WINDOW_CHUNKS = WINDOW // CHUNK
KEY_BLOCK = (WINDOW_CHUNKS + 1) * CHUNK
ROPE_DIM = HEAD_DIM // 4
ROPE_THETA = 500000.0

SG_BLOCK = 128
SG_GROUPS = 8
SG_WIDTH = 1024
SG_GROUP_WIDTH = SG_WIDTH // SG_GROUPS

N_BRANCHES = 2
IN_SIZES = [ATT_WIDTH, KV_WIDTH, KV_WIDTH, ATT_WIDTH,
            SG_WIDTH, SG_WIDTH, SG_WIDTH,
            N_BRANCHES * D_MODEL]
IN_WIDTH = int(sum(IN_SIZES))
IN_SPLITS_2 = [int(s) for s in np.cumsum(IN_SIZES)[:-1]]


def rmsnorm_2(x, g):
    xf = x.astype(jnp.float32)
    y = xf * lax.rsqrt(jnp.mean(xf * xf, axis=-1, keepdims=True) + EPS)
    return (y * g.astype(jnp.float32)).astype(x.dtype)

def layernorm(x, g, b):
    xf = x.astype(jnp.float32)
    mu = jnp.mean(xf, axis=-1, keepdims=True)
    xc = xf - mu
    y = xc * lax.rsqrt(jnp.mean(xc * xc, axis=-1, keepdims=True) + EPS)
    return (y * g.astype(jnp.float32) + b.astype(jnp.float32)).astype(x.dtype)

def partial_rope(x, pos):
    half = ROPE_DIM // 2
    inv_freq = ROPE_THETA ** (-(jnp.arange(half, dtype=jnp.float32) * 2.0) / ROPE_DIM)
    ang = pos.astype(jnp.float32)[:, None] * inv_freq[None, :]
    cos = jnp.cos(ang)[None, :, None, :]
    sin = jnp.sin(ang)[None, :, None, :]
    xf = x.astype(jnp.float32)
    x1, x2, rest = xf[..., :half], xf[..., half:ROPE_DIM], xf[..., ROPE_DIM:]
    out = jnp.concatenate([x1 * cos - x2 * sin, x2 * cos + x1 * sin, rest], axis=-1)
    return out.astype(x.dtype)

def window_sink_attention(q, k, v, sinks):
    B, S = q.shape[0], q.shape[1]
    nc = S // CHUNK
    qc = q.reshape(B, nc, CHUNK, ATT_KV_HEADS, ATT_GROUP, HEAD_DIM)
    pad = ((0, 0), (WINDOW_CHUNKS, 0), (0, 0), (0, 0), (0, 0))
    kc = jnp.pad(k.reshape(B, nc, CHUNK, ATT_KV_HEADS, HEAD_DIM), pad)
    vc = jnp.pad(v.reshape(B, nc, CHUNK, ATT_KV_HEADS, HEAD_DIM), pad)
    kb = jnp.concatenate([kc[:, j:j + nc] for j in range(WINDOW_CHUNKS + 1)], axis=2)
    vb = jnp.concatenate([vc[:, j:j + nc] for j in range(WINDOW_CHUNKS + 1)], axis=2)
    s = jnp.einsum('bnqhgd,bnkhd->bhgnqk', qc, kb,
                   preferred_element_type=jnp.float32) * (HEAD_DIM ** -0.5)
    key_chunk = jnp.arange(nc)[:, None] - WINDOW_CHUNKS + jnp.arange(WINDOW_CHUNKS + 1)[None, :]
    valid = jnp.repeat(key_chunk >= 0, CHUNK, axis=1)
    s = jnp.where(valid[None, None, None, :, None, :], s, -1e30)
    sink = sinks.astype(jnp.float32).reshape(ATT_KV_HEADS, ATT_GROUP)[None, :, :, None, None, None]
    m = jnp.maximum(jnp.max(s, axis=-1, keepdims=True), sink)
    p = jnp.exp(s - m)
    denom = jnp.sum(p, axis=-1, keepdims=True) + jnp.exp(sink - m)
    o = jnp.einsum('bhgnqk,bnkhd->bnqhgd', p / denom, vb.astype(jnp.float32))
    return o.reshape(B, S, ATT_WIDTH).astype(q.dtype)

def chunked_spatial_gating(u, v, w_s, b_s, ln_g, ln_b):
    B, S = u.shape[0], u.shape[1]
    nb = S // SG_BLOCK
    v = layernorm(v, ln_g, ln_b)
    vb = v.reshape(B, nb, SG_BLOCK, SG_GROUPS, SG_GROUP_WIDTH)
    cidx = np.arange(SG_BLOCK) // CHUNK
    mask = jnp.asarray(cidx[None, :] <= cidx[:, None])
    w = jnp.where(mask[None], w_s, jnp.zeros_like(w_s))
    mixed = jnp.einsum('gij,bnjgc->bnigc', w, vb) + jnp.transpose(b_s)[None, None, :, :, None]
    return u * mixed.reshape(B, S, SG_WIDTH)

def second_inputs(seed: int = 0) -> dict:
    key = jax.random.key(seed)
    ks = jax.random.split(key, 16)
    f32 = jnp.float32
    d = D_MODEL
    x = jax.random.normal(ks[0], (BATCH, SEQ, d), f32)
    norm_g = 1.0 + 0.05 * jax.random.normal(ks[1], (DEPTH, d), f32)
    w_in = jax.random.normal(ks[2], (DEPTH, d, IN_WIDTH), f32) * d ** -0.5
    b_merge = 0.01 * jax.random.normal(ks[3], (DEPTH, N_BRANCHES * d), f32)
    att_sinks = 0.5 * jax.random.normal(ks[4], (DEPTH, ATT_HEADS), f32)
    sg_w = jax.random.normal(ks[5], (DEPTH, SG_GROUPS, SG_BLOCK, SG_BLOCK), f32) * (0.5 * SG_BLOCK ** -0.5)
    sg_b = 1.0 + 0.1 * jax.random.normal(ks[6], (DEPTH, SG_GROUPS, SG_BLOCK), f32)
    sg_ln_g = 1.0 + 0.05 * jax.random.normal(ks[7], (DEPTH, SG_WIDTH), f32)
    sg_ln_b = 0.02 * jax.random.normal(ks[8], (DEPTH, SG_WIDTH), f32)
    w_att_out = jax.random.normal(ks[9], (DEPTH, ATT_WIDTH, d), f32) * ATT_WIDTH ** -0.5
    w_sg_out = jax.random.normal(ks[10], (DEPTH, SG_WIDTH, d), f32) * SG_WIDTH ** -0.5
    w_o = jax.random.normal(ks[11], (DEPTH, d, d), f32) * d ** -0.5
    final_g = 1.0 + 0.05 * jax.random.normal(ks[12], (d,), f32)
    return {"x": x, "norm_g": norm_g, "w_in": w_in, "b_merge": b_merge,
            "att_sinks": att_sinks, "sg_w": sg_w, "sg_b": sg_b, "sg_ln_g": sg_ln_g,
            "sg_ln_b": sg_ln_b, "w_att_out": w_att_out, "w_sg_out": w_sg_out,
            "w_o": w_o, "final_g": final_g}

def second_block(x, norm_g, w_in, b_merge, att_sinks, sg_w, sg_b, sg_ln_g, sg_ln_b,
              w_att_out, w_sg_out, w_o, final_g):
    B, S = x.shape[0], x.shape[1]
    pos = jnp.arange(S)
    for l in range(DEPTH):
        h = rmsnorm_2(x, norm_g[l])
        proj = h @ w_in[l]
        q, k, v, za, u, vs, zs, gm = jnp.split(proj, IN_SPLITS_2, axis=-1)
        q = partial_rope(q.reshape(B, S, ATT_HEADS, HEAD_DIM), pos)
        k = partial_rope(k.reshape(B, S, ATT_KV_HEADS, HEAD_DIM), pos)
        v = v.reshape(B, S, ATT_KV_HEADS, HEAD_DIM)
        a = window_sink_attention(q, k, v, att_sinks[l])
        a = (a * jax.nn.silu(za)) @ w_att_out[l]
        sgo = chunked_spatial_gating(jax.nn.gelu(u, approximate=False),
                                     jax.nn.gelu(vs, approximate=False),
                                     sg_w[l], sg_b[l], sg_ln_g[l], sg_ln_b[l])
        sgo = (sgo * jax.nn.silu(zs)) @ w_sg_out[l]
        ga, gs = jnp.split(jax.nn.sigmoid(gm + b_merge[l]), N_BRANCHES, axis=-1)
        y = ga * a + gs * sgo
        x = x + y @ w_o[l]
    return rmsnorm_2(x, final_g)


def setup_inputs(seed=0):
    out = dict(first_inputs(seed))
    for name, value in second_inputs(seed + 1).items():
        if name != "x":
            out[name + "_2"] = value
    return out


def reference(
    x, norm1_g, w_in, conv_a_w, ssm_conv_w, ssm_conv_b, ssm_dt_bias, ssm_a_log, ssm_d,
    ssm_norm_g, w_branch, w_o, norm2_g, w_gate_up, w_down, final_g, norm_g_2, w_in_2, b_merge_2,
    att_sinks_2, sg_w_2, sg_b_2, sg_ln_g_2, sg_ln_b_2, w_att_out_2, w_sg_out_2, w_o_2,
    final_g_2,
):
    x = first_block(
        x, norm1_g, w_in, conv_a_w, ssm_conv_w, ssm_conv_b, ssm_dt_bias, ssm_a_log, ssm_d,
        ssm_norm_g, w_branch, w_o, norm2_g, w_gate_up, w_down, final_g,
    )
    return second_block(
        x, norm_g_2, w_in_2, b_merge_2, att_sinks_2, sg_w_2, sg_b_2, sg_ln_g_2, sg_ln_b_2,
        w_att_out_2, w_sg_out_2, w_o_2, final_g_2,
    )


_drawn_inputs = setup_inputs


def setup_inputs(seed=0):
    import zlib

    import numpy as np

    out = dict(_drawn_inputs(seed))
    spreads = {}
    factors = {'ssm_conv_b': 4.486,
     'ssm_norm_g': 6.155,
     'norm2_g': 4.616,
     'final_g': 2.75,
     'norm_g_2': 3.039,
     'b_merge_2': 24.563,
     'att_sinks_2': 64.0,
     'sg_b_2': 2.889,
     'sg_ln_g_2': 8.0,
     'sg_ln_b_2': 28.96}
    for name, (base, spread) in spreads.items():
        noise = np.random.default_rng([zlib.crc32(name.encode()), seed]).standard_normal(out[name].shape)
        drawn = base * np.exp(spread * noise) if base else spread * noise
        out[name] = __import__('jax').numpy.asarray(drawn.astype(out[name].dtype))
    for name, factor in factors.items():
        out[name] = (out[name] * factor).astype(out[name].dtype)
    return out
```

```python
import numpy as np
import concourse.bass as bass
from concourse import mybir
from contextlib import ExitStack

SEQ, DM = 512, 1024
P = 128
KD = DM // P
TT = SEQ // P
HEADS, DH = 4, 64
BW = HEADS * DH
FFN = 2816
FT = FFN // P
FFN_PARTS = (8, 8, 6)
EPS = 1e-6
NEG = -1e30
UC = 256
KB = 1024

IN_XA, IN_BG, IN_CG = 0, BW, 2 * BW
IN_QB, IN_KB, IN_VB = 3 * BW, 4 * BW, 5 * BW
IN_Z, IN_X, IN_BC, IN_DT = 6 * BW, 7 * BW, 8 * BW, 9 * BW
IN_QD = IN_DT + HEADS
IN_KD, IN_VD = IN_QD + BW, IN_QD + 2 * BW
IN_G = IN_QD + 3 * BW
AH, GW = 16, 128
I2_Q, I2_K, I2_V, I2_ZA = 0, 1024, 1152, 1280
I2_U, I2_VS, I2_ZS, I2_GA, I2_GS = 2304, 3328, 4352, 5376, 6400

PAR = {}
_at = 0
for _n, _w in (("g1", 8), ("ca", 6), ("cw", 16), ("cb", 4), ("ng", 2), ("dsk", 2), ("g2", 8), ("fg", 8),
               ("ng2", 8), ("bm", 16), ("fg2", 8), ("sink", 16), ("dtb", 4), ("alog", 4),
               ("eps", 1)):
    PAR[_n] = (_at, _w)
    _at += _w
NPAR = _at

REG = [(0, 512), (512, 384), (896, 256), (1152, 128)]
RBANK = [(0, 0), (1, 0), (2, 0), (1, 384)]
QREG = [(1152, 128), (896, 256), (512, 384), (0, 512)]
QBANK = [(1, 384), (2, 0), (1, 0), (0, 0)]
BANKS = [(0, 512, 0), (1, 512, 512), (2, 256, 0)]
RUNS = [(0, 0, 0, 512), (1, 0, 512, 384), (2, 0, 896, 256), (1, 384, 1152, 128)]


def build_program(nc, x, par, cst1, cst2a, cst2b, w_in, w_branch, w_o, w_gu, w_down, w_in2, sg_w, sg_b, ln_g,
                  ln_b, w_ao, w_so, w_o2, out):
    f32, f32r = mybir.dt.float32, mybir.dt.float32r
    ALU, ACT = mybir.AluOpType, mybir.ActivationFunctionType
    AX = mybir.AxisListType
    EXP_LN = "natural_log_exp_and_others"

    ctx = ExitStack()
    with ctx:
        base = (nc.sbuf_base + 31) // 32 * 32

        def place(name, shape, kb, dt=f32):
            return nc.alloc_sbuf_tensor_at(name, shape, dt, offset=base + int(kb * KB))

        sems = {}

        def sem(name):
            if name not in sems:
                sems[name] = ctx.enter_context(nc.semaphore(name))
            return sems[name]

        raw = place("raw", [P, 2, 8, UC], 0)
        whi = place("whi", [P, 2, 8, UC], 16, f32r)
        wlo = place("wlo", [P, 2, 8, UC], 32, f32r)
        raw_b = place("raw_b", [P, 2, 2, UC], 48)
        whi_b = place("whi_b", [P, 2, 2, UC], 52, f32r)
        wlo_b = place("wlo_b", [P, 2, 2, UC], 56, f32r)
        xT = place("xT", [P, KD, SEQ], 60)
        hh = place("hh", [P, KD, SEQ], 76, f32r)
        hl = place("hl", [P, KD, SEQ], 92, f32r)
        c1 = place("c1", [P, 1024], 108)
        prm = place("prm", [P, NPAR], 112)
        sml = place("sml", [P, 256], 113)
        R = place("R", [P, SEQ], 114)
        Z0 = 116.0
        xtm = place("xtm", [P, TT, DM], Z0)
        xa = place("xa", [P, 2, SEQ], Z0)
        bgate = place("bgate", [P, 2, SEQ], Z0 + 4)
        cbuf = place("cbuf", [P, 2, SEQ + 2], Z0 + 8)
        merged = place("merged", [P, KD, SEQ], Z0)
        yh = [place(f"yh{i}", [P, 2, SEQ], Z0 + 16 + 8 * i, f32r) for i in range(2)]
        yl = [place(f"yl{i}", [P, 2, SEQ], Z0 + 20 + 8 * i, f32r) for i in range(2)]
        U0 = Z0 + 32
        mh = place("mh", [P, KD, SEQ], U0, f32r)
        ml = place("ml", [P, KD, SEQ], U0 + 16, f32r)
        xs = place("xs", [P, 2, SEQ], U0)
        bm = place("bmat", [P, SEQ], U0 + 4)
        cm = place("cmat", [P, SEQ], U0 + 6)
        sz = place("sz", [P, 2, SEQ], U0 + 8)
        xdt = place("xdt", [P, TT, BW], U0 + 12)
        qd = place("qd", [P, 2, SEQ], U0 + 16)
        kd = place("kd", [P, 2, SEQ], U0 + 20)
        vd = place("vd", [P, TT, BW], U0 + 24)
        adtb = place("adtb", [P, TT, P], U0 + 28)
        ydh = place("ydh", [P, 2, SEQ], U0, f32r)
        ydl = place("ydl", [P, 2, SEQ], U0 + 4, f32r)
        qb = place("qb", [P, 2, SEQ], Z0 + 64)
        kb = place("kb", [P, 2, SEQ], Z0 + 68)
        vb = place("vb", [P, TT, BW], Z0 + 72)
        T0 = Z0 + 76
        gt = place("gt", [P, 2, SEQ], T0)
        xbuf = place("xbuf", [P, 4, SEQ + 3], T0)
        etmp = place("etmp", [P, SEQ], T0 + 8.25)
        sqjunk = place("sqjunk", [P, DM], T0)
        cbs = place("cbs", [P, 1280], T0 + 4)
        dec = place("dec", [P, 1280], T0 + 9)
        stl = place("stl", [P, 1280], T0 + 4)
        stsp = place("stsp", [P, 1280], T0 + 9)
        mp = place("mp", [P, 1280], T0 + 4)
        mpt = place("mpt", [P, 1280], T0 + 9)
        msq = place("msq", [P, 2, SEQ], Z0 + 28)
        mrs = place("mrs", [P, 2, SEQ], Z0 + 24)
        acc0 = place("acc0", [P, SEQ], Z0)
        sq0 = place("sq0", [P, 2, SEQ], Z0 + 2)
        ah = place("ah", [P, 8, SEQ], Z0, f32r)
        al = place("al", [P, 8, SEQ], Z0 + 16, f32r)
        fg_t = place("fg_t", [P, 2, SEQ], Z0 + 64)
        fu_t = place("fu_t", [P, 2, SEQ], Z0 + 68)
        acc1 = place("acc1", [P, SEQ], Z0 + 32)
        acc2 = place("acc2", [P, SEQ], Z0 + 34)
        sq1 = place("sq1", [P, 2, SEQ], Z0 + 36)
        sq2 = place("sq2", [P, 2, SEQ], Z0 + 40)
        r1 = place("r1", [P, SEQ], Z0 + 44)
        r2 = place("r2", [P, SEQ], Z0 + 46)
        cs2 = place("cs2", [P, 2, SEQ], 48)
        lng = place("lng", [P, DM], 52)
        lnb = place("lnb", [P, DM], 56)
        ath = place("ath", [P, KD, SEQ], Z0, f32r)
        atl = place("atl", [P, KD, SEQ], Z0 + 16, f32r)
        sgh = place("sgh", [P, KD, SEQ], Z0, f32r)
        sgl = place("sgl", [P, KD, SEQ], Z0 + 16, f32r)
        vg = place("vg", [P, TT, DM], Z0 + 32)
        rope_q = place("rope_q", [P, 2, SEQ], Z0 + 32)
        rope_t = place("rope_t", [P, 2, SEQ], Z0 + 36)
        za_e = place("za_e", [P, 2, SEQ], Z0 + 40)
        y2 = place("y2", [P, KD, SEQ], Z0 + 48)
        q2 = place("q2", [P, 4, SEQ], Z0 + 48)
        za = place("za", [P, 4, SEQ], Z0 + 56)
        k2 = place("k2", [P, 2, SEQ], Z0 + 64)
        v2 = place("v2", [P, TT, GW], Z0 + 68)
        wp = place("wp", [P, 3, 2, 256], Z0 + 70)
        wpt = place("wpt", [P, 2, SEQ], Z0 + 76)
        att_t = place("att_t", [P, SEQ], Z0 + 80)
        g2t = place("g2t", [P, 2, SEQ], Z0 + 64)
        ub = place("ub", [P, 2, SEQ], Z0 + 64)
        zb = place("zb", [P, 2, SEQ], Z0 + 68)
        sgt = place("sgt", [P, 2, SEQ], Z0 + 72)
        y2h = place("y2h", [P, KD, SEQ], Z0 + 32, f32r)
        y2l = place("y2l", [P, KD, SEQ], Z0 + 64, f32r)
        D0 = Z0 + 82.25
        perm = place("perm", [P, P + 256], D0)
        bsb = place("bsb", [P, 8, P], D0 + 1.5)
        wT = place("wT", [P, 8, P], D0 + 5.5)
        sgw = place("sgw", [P, 8, P], Z0 + 70)
        g4t = place("g4t", [P, 2, SEQ], D0 + 1.5)
        acc3 = place("acc3", [P, SEQ], Z0)
        sq3 = place("sq3", [P, 2, SEQ], Z0 + 2)
        fo = place("fo", [P, 2, SEQ], Z0 + 8)
        ot = place("ot", [P, TT, DM], Z0 + 16)
        dtf = place("dtf", [HEADS, SEQ], Z0 + 28)
        wdt = place("wdt", [P, KD, HEADS], Z0 + 24)
        wdth = place("wdth", [P, KD, HEADS], Z0 + 25, f32r)
        wdtl = place("wdtl", [P, KD, HEADS], Z0 + 26, f32r)

        ident = c1[:, 0:128]
        upper = c1[:, 128:640]
        u_incl = c1[:, 128:256]
        ones = c1[:, 256:384]
        u_strict = c1[:, 640:768]
        t_after = c1[:, 768:896]
        negmask = c1[:, 896:1024]

        def pcol(name, i, n=1):
            return prm[:, PAR[name][0] + i:PAR[name][0] + i + n]

        ss = sml[:, 0:4]
        rcol = sml[:, 4:8]
        dtv = sml[:, 8:24]
        dta = sml[:, 24:40]
        dts = sml[:, 40:56]
        dts2 = sml[:, 56:72]
        dtq = sml[:, 72:88]
        adt = sml[:, 88:104]
        acs = sml[:, 104:120]
        ealog = sml[:, 120:124]
        fgng = sml[:, 124:132]
        mmx = sml[:, 132:136]
        mnm = sml[:, 136:140]
        mls = sml[:, 140:144]
        mrl = sml[:, 144:148]
        wmx = sml[:, 148:154]
        wnm = sml[:, 154:160]
        wls = sml[:, 160:166]
        wes = sml[:, 166:172]
        bns = sml[:, 172:220]
        mv = sml[:, 220:228]
        lrs = sml[:, 228:232]
        dte = sml[:, 232:248]

        G = [ctx.enter_context(nc.psum_tensor(f"gemm{i}", [P, 512], f32)) for i in range(4)]
        M = [ctx.enter_context(nc.psum_tensor(f"mix{i}", [P, 512], f32)) for i in range(4)]

        def as_f32(ap):
            return ap.bitcast(f32)

        def cols(w, c0, n, k0=0, k=KD):
            return w[k0 * P:(k0 + k) * P, c0:c0 + n].rearrange("(k p) c -> p k c", p=P)

        N_A = 12
        ORDER = (0, 2, 3, 1)
        N_B = 16
        n_b0, n_c0 = N_A, N_A + N_B
        n_d0 = n_c0 + 4
        ffn_units = []
        _n, _h = n_d0, 0
        for part in FFN_PARTS:
            ffn_units.append((_n, part, _h))
            _n += part + 4
            _h += part
        n_e0 = _n
        n_qz = n_e0 + 1
        n_vs = n_qz + 8
        n_ga = n_vs + 4
        n_uz = n_ga + 8
        n_gs = n_uz + 8
        n_o2 = n_gs + 8
        N_UNITS = n_o2 + 4

        def tiles_before(n):
            return 2 * n + 2 * min(max(n - n_b0, 0), N_B)

        def raw_count(n):
            def dmas(m):
                two = n_b0 <= m < n_c0 or any(a <= m < a + h for a, h, _ in ffn_units)
                return 2 if two else 1
            return 16 * sum(dmas(m) for m in range(n % 2, n + 1, 2))

        block = ctx.enter_context(nc.Block())

        @block.sync
        def _(sp):
            sp.dma_start(ident, cst1[:, 0:P]).then_inc(sem("ident_in"), 16)
            sp.dma_start(prm[:, :], par).then_inc(sem("par_in"), 16)
            for q in range(4):
                sp.dma_start(xtm[:, :, q * 256:(q + 1) * 256],
                             x[:, q * 256:(q + 1) * 256].rearrange("(t p) c -> p t c", p=P)).then_inc(sem(f"x_in{q}"), 16)

            def load(n, src, dst=None):
                sp.dma_start(raw[:, n % 2] if dst is None else dst, src).then_inc(sem(f"raw_in{n % 2}"), 16)

            def slot_free(n):
                if n >= 2:
                    sp.wait_ge(sem("lo_done"), n - 1)

            a_cols = (IN_XA, IN_BG, IN_CG, IN_X, IN_BC, IN_Z, IN_QD, IN_KD, IN_VD, IN_QB, IN_KB, IN_VB)
            for n, c in enumerate(a_cols):
                slot_free(n)
                load(n, cols(w_in, c, UC))
                if n == 0:
                    sp.dma_start(c1[:, P:], cst1[:, P:]).then_inc(sem("c1_in"), 16)
                if n == 1:
                    sp.dma_start(wdt[:, :, :], cols(w_in, IN_DT, HEADS)).then_inc(sem("wdt_in"), 16)
            for i in range(N_B):
                n, br, p = n_b0 + i, ORDER[i // 4], i % 4
                slot_free(n)
                load(n, cols(w_in, IN_G + br * DM + p * UC, UC))
                load(n, cols(w_branch[br], p * UC, UC, 0, 2), raw_b[:, n % 2])
            for p in range(4):
                slot_free(n_c0 + p)
                load(n_c0 + p, cols(w_o, p * UC, UC))
                if p == 1:
                    sp.wait_ge(sem("tile_done"), tiles_before(n_c0))
                    sp.dma_start(cs2[:, :, :], cst2a.rearrange("p (a s) -> p a s", a=2)).then_inc(sem("c2_in"), 16)
                    sp.dma_start(lng[:, :], ln_g.partition_broadcast(P)).then_inc(sem("c2_in"), 16)
                    sp.dma_start(lnb[:, :], ln_b.partition_broadcast(P)).then_inc(sem("c2_in"), 16)
                    sp.wait_ge(sem("m_lo"), KD)
                    sp.dma_start(perm[:, :], cst2b).then_inc(sem("c2_in"), 16)
                    sp.dma_start(bsb[:, :, :].rearrange("p g i -> p (g i)"), sg_b.partition_broadcast(P)).then_inc(sem("c2_in"), 16)
            for n0, part, h0 in ffn_units:
                for j in range(part):
                    n, h = n0 + j, h0 + j
                    slot_free(n)
                    load(n, cols(w_gu, h * P, P), raw[:, n % 2, :, 0:P])
                    load(n, cols(w_gu, FFN + h * P, P), raw[:, n % 2, :, P:UC])
                for p in range(4):
                    n = n0 + part + p
                    slot_free(n)
                    load(n, cols(w_down, p * UC, UC, h0, part), raw[:, n % 2, 0:part])
            slot_free(n_e0)
            load(n_e0, cols(w_in2, I2_K, UC))
            sp.wait_ge(sem("tile_done"), tiles_before(n_e0))
            sp.dma_start(sgw[:, :, :], sg_w.rearrange("g i j -> i g j")).then_inc(sem("sgw_in"), 16)
            for p in range(4):
                for i, c in enumerate((I2_Q, I2_ZA)):
                    n = n_qz + 2 * p + i
                    slot_free(n)
                    load(n, cols(w_in2, c + p * UC, UC))
            for p in range(4):
                slot_free(n_vs + p)
                load(n_vs + p, cols(w_in2, I2_VS + p * UC, UC))
            for n0, pair in ((n_ga, ((w_in2, I2_GA), (w_ao, 0))), (n_uz, ((w_in2, I2_U), (w_in2, I2_ZS))),
                             (n_gs, ((w_in2, I2_GS), (w_so, 0)))):
                for p in range(4):
                    for i, (w, c) in enumerate(pair):
                        slot_free(n0 + 2 * p + i)
                        load(n0 + 2 * p + i, cols(w, c + p * UC, UC))
            for p in range(4):
                slot_free(n_o2 + p)
                load(n_o2 + p, cols(w_o2, p * UC, UC))
            for q in range(4):
                sp.wait_ge(sem("o_copied"), 2 * q + 2)
                sp.dma_start(out[:, q * 256:(q + 1) * 256].rearrange("(t p) c -> p t c", p=P),
                             ot[:, :, q * 256:(q + 1) * 256]).then_inc(sem("o_out"), 16)
            sp.wait_ge(sem("o_out"), 64)

        @block.gpsimd
        def _(pool):
            def rest(n, s, with_b=False):
                pool.wait_ge(sem("hi_done"), n + 1)
                a = lambda t: t[:, s].rearrange("p k c -> p (k c)")
                if with_b:
                    nc.gpsimd.tensor_tensor(a(wlo_b), a(raw_b), as_f32(a(whi_b)), ALU.subtract)
                nc.gpsimd.tensor_tensor(a(wlo), a(raw), as_f32(a(whi)), ALU.subtract).then_inc(sem("lo_done"), 1)

            def rests(n0, n1, with_b=False):
                if (n1 - n0) // 2:
                    with pool.Fori(0, (n1 - n0) // 2) as i:
                        for s in range(2):
                            rest(2 * i + n0 + s, (n0 + s) % 2, with_b)
                if (n1 - n0) % 2:
                    rest(n1 - 1, (n1 - 1) % 2, with_b)

            rests(0, n_b0)
            rests(n_b0, n_c0, True)
            rests(n_c0, N_UNITS)

        MIX = {6: [("dt",)], 8: [("dtT",)], 13: [("xsT",)], 14: [("acs",)], 15: [("cb", 0)], 16: [("mh1", 0)],
               17: [("mh2", 0), ("mh1", 1)], 18: [("mh2", 1), ("cb", 1)], 19: [("mh1", 2)],
               20: [("mh2", 2), ("mh1", 3)], 21: [("mh2", 3)], 22: [("mn", 0)], 23: [("mn", 1)]}
        for h in range(HEADS):
            for slots, st in (((25 + 2 * h, 26 + 2 * h, 27 + 2 * h), "mo"), ((34 + 3 * h, 36 + 3 * h, 37 + 3 * h), "st")):
                for i, at in enumerate(slots):
                    step = (f"{st}{i + 1}", h)
                    if i == 2:
                        MIX.setdefault(at, []).insert(0, step)
                    else:
                        MIX.setdefault(at, []).append(step)

        def run_mix(stages, slot):
            for name, *args in MIX.get(slot, []):
                stages[name](*args)

        @block.tensor
        def _(pe):
            mm = nc.tensor.matmul

            def gemm_fm(T, n, s, xh, xl, kts, col, first, whi_=whi, wlo_=wlo, hook=None, ready=None):
                bank = G[T % 4] if isinstance(T, int) else G[T[1]]
                Tv = T if isinstance(T, int) else T[0]
                if not isinstance(T, int) or T >= 4:
                    pe.wait_ge(sem("tile_free"), Tv - 3)
                if first:
                    pe.wait_ge(sem("hi_done"), n + 1)
                half = (3 * kts // 2 + 1) // 2
                for k in range(kts):
                    if ready:
                        pe.wait_ge(sem(ready[0]), ready[1] + k + 1)
                    w = whi_[:, s, k, col:col + P]
                    mm(bank[:, :], w, xh[:, k, :], start=(k == 0), stop=False)
                    mm(bank[:, :], w, xl[:, k, :], start=False, stop=False)
                    if hook and k == half - 1:
                        hook()
                if first:
                    pe.wait_ge(sem("lo_done"), n + 1)
                for k in range(kts):
                    last = mm(bank[:, :], wlo_[:, s, k, col:col + P], xh[:, k, :], start=False, stop=(k == kts - 1))
                last.then_inc(sem("tile_done"), 1)

            def gemm_tm(T, n, c0, w_cols, per_bank, hook=None):
                bank, s = G[T % 4], n % 2
                pe.wait_ge(sem("tile_free"), T - 3)
                pe.wait_ge(sem("hi_done"), n + 1)
                pe.wait_ge(sem("lo_done"), n + 1)
                for i in range(per_bank):
                    t = i if per_bank == TT else (T % 2) * per_bank + i
                    o = bank[:, i * w_cols:(i + 1) * w_cols]
                    for k in range(KD):
                        w, tok = slice(c0, c0 + w_cols), slice(t * P, (t + 1) * P)
                        mm(o, hh[:, k, tok], whi[:, s, k, w], start=(k == 0), stop=False)
                        mm(o, hl[:, k, tok], whi[:, s, k, w], start=False, stop=False)
                        last = mm(o, hh[:, k, tok], wlo[:, s, k, w], start=False, stop=(k == KD - 1))
                    if i == per_bank - 1:
                        last.then_inc(sem("tile_done"), 1)
                    if hook:
                        hook()

            def unit_fm(n, xh=hh, xl=hl, kts=KD, after=None, hook=None, ready=None):
                for j in range(2):
                    gemm_fm(tiles_before(n) + j, n, n % 2, xh, xl, kts, j * P, j == 0, hook=hook,
                            ready=None if j else ready)
                    if after:
                        after(j)

            pe.wait_ge(sem("ident_in"), 16)
            for m in range(KD):
                pe.wait_ge(sem(f"x_in{m // 2}"), 16)
                for t in range(TT):
                    last = nc.tensor.transpose((G + M)[m][:, t * P:(t + 1) * P], xtm[:, t, m * P:(m + 1) * P], ident)
                last.then_inc(sem("xT_ps"), 1)

            def st_dt():
                pe.wait_ge(sem("wdt_lo"), 1)
                for k in range(KD):
                    o = M[0][0:HEADS, :]
                    mm(o, wdth[:, k, :], hh[:, k, :], start=(k == 0), stop=False)
                    mm(o, wdth[:, k, :], hl[:, k, :], start=False, stop=False)
                    last = mm(o, wdtl[:, k, :], hh[:, k, :], start=False, stop=(k == KD - 1))
                last.then_inc(sem("dt_ps"), 1)

            def st_dtT():
                pe.wait_ge(sem("dt_f"), 1)
                for t in range(TT):
                    last = nc.tensor.transpose(M[0][:, t * HEADS:(t + 1) * HEADS], dtf[0:HEADS, t * P:(t + 1) * P],
                                               ident[0:HEADS, 0:HEADS])
                last.then_inc(sem("dtT_ps"), 1)

            def st_xsT():
                pe.wait_ge(sem("silu"), 2)
                for b in range(2):
                    for i in range(2):
                        for f in range(2):
                            t = 2 * b + i
                            last = nc.tensor.transpose(M[1 + b][:, i * BW + f * P:i * BW + (f + 1) * P],
                                                       xs[:, f, t * P:(t + 1) * P], ident)
                    last.then_inc(sem("xsT_ps"), 1)

            def st_acs():
                pe.wait_ge(sem("adt"), 1)
                for n in range(TT):
                    o = M[3][:, n * HEADS:(n + 1) * HEADS]
                    for m in range(n + 1):
                        last = mm(o, u_incl if m == n else ones, adt[:, m * HEADS:(m + 1) * HEADS],
                                  start=(m == 0), stop=(m == n))
                last.then_inc(sem("acs_ps"), 1)

            def st_cb(g):
                pe.wait_ge(sem("silu"), 4)
                if g == 0:
                    pe.wait_ge(sem("dtv_read"), 1)
                    pe.wait_ge(sem("xdt"), 2)
                else:
                    pe.wait_ge(sem("y_mid"), 1)
                gs = slice(64 * g, 64 * g + 64)
                for n, (_, w) in enumerate(REG):
                    b, c = RBANK[n]
                    last = mm(M[b][:, c:c + w], bm[gs, n * P:(n + 1) * P], cm[gs, n * P:SEQ], start=True, stop=True)
                last.then_inc(sem("cb_ps"), 1)

            def st_mh1(h):
                pe.wait_ge(sem("adtb"), h + 1)
                if h == 0:
                    pe.wait_ge(sem("acs"), 1)
                else:
                    pe.wait_ge(sem("seg"), h)
                for m in range(TT):
                    last = mm(M[3][:, m * P:SEQ], adtb[:, m, :], upper[:, 0:SEQ - m * P], start=(m == 0), stop=(m == TT - 1))
                last.then_inc(sem("acsb_ps"), 1)

            def st_mh2(h):
                pe.wait_ge(sem("mt"), h + 1)
                if h % 2 == 0:
                    pe.wait_ge(sem("cbs"), h // 2 + 1)
                o = M[0][64 * (h % 2):64 * (h % 2) + 64, :]
                for n, (a, w) in enumerate(REG):
                    last = mm(o[:, n * P:SEQ], xdt[:, n, h * DH:(h + 1) * DH], dec[:, a:a + w],
                              start=(n == 0), stop=(n == TT - 1))
                last.then_inc(sem("y_ps"), 1)

            def st_mn(g):
                pe.wait_ge(sem("y_sq"), g + 1)
                if g:
                    pe.wait_ge(sem("yrstd"), g)
                mm(M[1][:, :], ones, msq[:, g, :], start=True, stop=True).then_inc(sem("ysum_ps"), 1)

            def st_mo1(h):
                if h == 0:
                    pe.wait_ge(sem("tile_free"), tiles_before(9))
                    pe.wait_ge(sem("yc_lo"), 2)
                else:
                    pe.wait_ge(sem("mo_pt"), 3 * h)
                r, t = slice(64 * (h % 2), 64 * (h % 2) + 64), h // 2
                for c in (3, 2, 0, 1):
                    b, o = QBANK[c]
                    w = (c + 1) * P
                    mm(M[b][:, o:o + w], qd[r, t, c * P:(c + 1) * P], kd[r, t, 0:w], start=True, stop=False)
                    last = mm(M[b][:, o + c * P:o + w], ident, negmask, start=False, stop=True)
                last.then_inc(sem("mo_s"), 1)

            def st_mo2(h):
                pe.wait_ge(sem("mo_p"), h + 1)
                for n in (0, 1, 3, 2):
                    b, o = RBANK[n]
                    for c in range(n, TT):
                        a = QREG[c][0] + n * P
                        last = nc.tensor.transpose(M[b][:, o + (c - n) * P:o + (c - n + 1) * P], mp[:, a:a + P], ident)
                last.then_inc(sem("mo_t"), 1)

            def attend(o, v, probs, h, done):
                for n, (a, w) in enumerate(REG):
                    last = mm(o[:, n * P:SEQ], v[:, n, h * DH:(h + 1) * DH], probs[:, a:a + w],
                              start=(n == 0), stop=(n == TT - 1))
                last.then_inc(sem(done), 1)

            def st_mo3(h):
                pe.wait_ge(sem("mo_pt"), 3 * h + 3)
                if h == 2:
                    pe.wait_ge(sem("yd_lo"), 1)
                attend(M[3][64 * (h % 2):64 * (h % 2) + 64, :], vd, mpt, h, "mo_o")

            def st_st1(h):
                if h == 0:
                    pe.wait_ge(sem("tile_free"), tiles_before(12))
                    pe.wait_ge(sem("yd_lo"), 2)
                else:
                    pe.wait_ge(sem("st_arg"), h)
                r, t = slice(64 * (h % 2), 64 * (h % 2) + 64), h // 2
                for n in (0, 1, 3, 2):
                    b, o = RBANK[n]
                    last = mm(M[b][:, o:o + REG[n][1]], kb[r, t, n * P:(n + 1) * P], qb[r, t, n * P:SEQ], start=True, stop=True)
                last.then_inc(sem("st_z"), 1)

            def st_st2(h):
                pe.wait_ge(sem("st_sp"), h + 1)
                for n in (0, 1, 3, 2):
                    b, o = RBANK[n]
                    a, w = REG[n]
                    last = mm(M[b][:, o:o + w], t_after, stsp[:, a:a + w], start=True, stop=(n == TT - 1))
                    for m in range(n + 1, TT):
                        a, w = REG[m]
                        last = mm(M[b][:, o + (m - n) * P:o + REG[n][1]], ones, stsp[:, a:a + w],
                                  start=False, stop=(m == TT - 1))
                last.then_inc(sem("st_b"), 1)

            def st_st3(h):
                pe.wait_ge(sem("st_w"), h + 1)
                if h == 2:
                    pe.wait_ge(sem("yb_lo"), 1)
                attend(M[3][64 * (h % 2):64 * (h % 2) + 64, :], vb, stl, h, "st_o")

            stages = {"dt": st_dt, "dtT": st_dtT, "xsT": st_xsT, "acs": st_acs, "cb": st_cb, "mh1": st_mh1, "mh2": st_mh2,
                      "mn": st_mn, "mo1": st_mo1, "mo2": st_mo2, "mo3": st_mo3, "st1": st_st1, "st2": st_st2,
                      "st3": st_st3}

            pe.wait_ge(sem("xg_kept"), 4)
            for n in range(N_A):
                def after(j, n=n):
                    if n == 0 and j == 1:
                        pe.wait_ge(sem("c1_in"), 16)
                        pe.wait_ge(sem("h_lo"), KD)
                        pe.wait_ge(sem("x_kept"), KD - 4)
                        pe.wait_ge(sem("rdiag"), 1)
                        for t in range(TT):
                            last = mm(M[0][:, t * P:(t + 1) * P], ones, xbuf[:, t, 0:P], start=True, stop=True)
                        last.then_inc(sem("r_ps"), 1)
                    run_mix(stages, 2 * n + j)
                if n in (8, 11):
                    for j in range(2):
                        gemm_tm(tiles_before(n) + j, n, 0, BW, 2)
                        after(j)
                else:
                    unit_fm(n, after=after, ready=("h_lo", 0) if n == 0 else None)

            for i in range(N_B):
                n = n_b0 + i
                s = n % 2
                yhi, ylo = ((yh[0], yl[0]), (yh[1], yl[1]), (ydh, ydl), (yh[0], yl[0]))[i // 4]
                for j in range(2):
                    T = tiles_before(n) + 2 * j
                    gemm_fm(T, n, s, hh, hl, KD, j * P, j == 0)
                    if i % 4 == 0 and j == 0:
                        pe.wait_ge(sem(("ya_lo", "yc_lo", "yd_lo", "yb_lo")[i // 4]), 2)
                    gemm_fm(T + 1, n, s, yhi, ylo, 2, j * P, False, whi_b, wlo_b)
                    run_mix(stages, 24 + 2 * i + j)

            for p in range(4):
                unit_fm(n_c0 + p, mh, ml, ready=None if p else ("m_lo", 0))

            for f, (n0, part, h0) in enumerate(ffn_units):
                if f == 0:
                    gemm_fm(tiles_before(n0), n0, n0 % 2, hh, hl, KD, 0, True, ready=("h2_lo", 0))
                    pe.wait_ge(sem("acc0"), KD)
                    mm(M[0][:, :], ones, acc0[:, :], start=True, stop=True).then_inc(sem("n2_ps"), 1)
                    gemm_fm(tiles_before(n0) + 1, n0, n0 % 2, hh, hl, KD, P, False)
                    unit_fm(n0 + 1)
                with pe.Fori(1 if f == 0 else 0, part // 2) as i:
                    for s in range(2):
                        n = 2 * i + n0 + s
                        for j in range(2):
                            b = (tiles_before(n0) + 2 * s + j) % 4
                            gemm_fm((4 * i + tiles_before(n0) + 2 * s + j, b), n, (n0 + s) % 2, hh, hl, KD, j * P, j == 0)
                for p in range(4):
                    unit_fm(n0 + part + p, ah, al, part, ready=None if p else ("act_lo", h0))

            T = tiles_before(n_e0)
            gemm_fm(T, n_e0, n_e0 % 2, hh, hl, KD, 0, True, ready=("h3_lo", 0))
            pe.wait_ge(sem("acc2"), KD)
            mm(M[0][:, :], ones, acc1[:, :], start=True, stop=True)
            mm(M[1][:, :], ones, acc2[:, :], start=True, stop=True).then_inc(sem("n3_ps"), 1)
            gemm_tm(T + 1, n_e0, P, GW, TT)

            def turn_rows():
                pe.wait_ge(sem("R3"), 1)
                for t in range(TT):
                    last = nc.tensor.transpose(M[2][:, t * P:(t + 1) * P], R[:, t * P:(t + 1) * P], ident)
                last.then_inc(sem("rcol_ps"), 1)
                pe.wait_ge(sem("sgw_in"), 16)
                for g in range(8):
                    last = nc.tensor.transpose(M[g // 4][:, (g % 4) * P:(g % 4 + 1) * P], sgw[:, g, :], ident)
                last.then_inc(sem("wT_ps"), 1)

            def turn_keys():
                pe.wait_ge(sem("tile_free"), tiles_before(n_e0) + 1)
                mm(M[3][:, :], perm[:, 0:P], rope_q[:, 0, :], start=True, stop=True).then_inc(sem("rope_ps"), 1)

            STEPS = KD * TT
            pos = [0]

            def keys_of(c):
                return (1,) if c == 0 else (0, 1)

            def w_scores(s):
                m, c = s // TT, s % TT
                if s % 8 == 0:
                    pe.wait_ge(sem("tile_free"), tiles_before(n_qz + s // 4) + 2)
                if s == 0:
                    pe.wait_ge(sem("k_ready"), 1)
                if s >= 1:
                    pe.wait_ge(sem("w_s"), s)
                kv = m // 4
                for h in range(2):
                    r = slice(64 * h, 64 * h + 64)
                    k0 = max(c - 1, 0) * P
                    o = P if c == 0 else 0
                    last = mm(M[h][:, o:256], q2[r, m % 4, c * P:(c + 1) * P], k2[r, kv, k0:(c + 1) * P],
                              start=True, stop=True)
                last.then_inc(sem("w_ps"), 1)

            def w_turn(s):
                m, c = s // TT, s % TT
                pe.wait_ge(sem("w_p"), s + 1)
                if s >= 1:
                    pe.wait_ge(sem("w_pt"), s)
                for h in range(2):
                    for kb_ in keys_of(c):
                        last = nc.tensor.transpose(M[2][:, (2 * h + kb_) * P:(2 * h + kb_ + 1) * P],
                                                   wp[:, s % 3, h, kb_ * P:(kb_ + 1) * P], ident)
                last.then_inc(sem("w_t"), 1)

            def w_values(s):
                m, c = s // TT, s % TT
                pe.wait_ge(sem("w_pt"), s + 1)
                if c == 0 and m >= 1:
                    pe.wait_ge(sem("w_o"), m)
                kv = m // 4
                for h in range(2):
                    for kb_ in keys_of(c):
                        last = mm(M[3][64 * h:64 * h + 64, c * P:(c + 1) * P], v2[:, c - 1 + kb_, kv * DH:(kv + 1) * DH],
                                  wpt[:, s % 2, (2 * h + kb_) * P:(2 * h + kb_ + 1) * P],
                                  start=(kb_ == keys_of(c)[0]), stop=(kb_ == 1))
                last.then_inc(sem("w_v"), 1)

            def w_slot(limit):
                i = pos[0]
                if i >= limit + 3:
                    return
                if 0 <= i - 3 < STEPS:
                    w_values(i - 3)
                if 0 <= i - 2 < STEPS:
                    w_turn(i - 2)
                if i < min(limit, STEPS):
                    w_scores(i)
                    pos[0] += 1
                elif limit == STEPS:
                    pos[0] += 1

            for p in range(4):
                n = n_qz + 2 * p
                lim = 8 * p
                for u in range(2):
                    for j in range(2):
                        gemm_fm(tiles_before(n + u) + j, n + u, (n + u) % 2, hh, hl, KD, j * P, j == 0,
                                hook=lambda: w_slot(lim))
                        if p == 0 and u == 0:
                            (turn_rows, turn_keys)[j]()
                        if u == 1 and j == 0:
                            for i in range(2):
                                pe.wait_ge(sem("rope_in"), 2 * p + i + 1)
                                mm(G[(tiles_before(n) + i) % 4][:, :], perm[:, 0:P], rope_q[:, i, :],
                                   start=True, stop=True).then_inc(sem("rope_ps"), 1)
                        w_slot(lim)
            for p in range(4):
                n = n_vs + p
                for j in range(2):
                    gemm_tm(tiles_before(n) + j, n, 0, UC, 2, hook=lambda: w_slot(STEPS))
            while pos[0] < STEPS + 3:
                w_slot(STEPS)

            for p in range(4):
                unit_fm(n_ga + 2 * p)
                unit_fm(n_ga + 2 * p + 1, ath, atl, ready=None if p else ("at_lo", 0))

            for p in range(4):
                unit_fm(n_uz + 2 * p)
                if p == 0:
                    pe.wait_ge(sem("vb_ready"), TT)
                    pe.wait_ge(sem("wT_ready"), 1)
                for j in range(2):
                    m = 2 * p + j
                    if m >= 2:
                        pe.wait_ge(sem("mixed"), m - 1)
                    for t in range(TT):
                        last = mm(M[m % 2][:, t * P:(t + 1) * P], vg[:, t, m * P:(m + 1) * P], wT[:, m, :],
                                  start=True, stop=True)
                    last.then_inc(sem("mixed_ps"), 1)
                unit_fm(n_uz + 2 * p + 1)
            for p in range(4):
                unit_fm(n_gs + 2 * p)
                unit_fm(n_gs + 2 * p + 1, sgh, sgl, ready=None if p else ("sg_lo", 0))

            for p in range(4):
                unit_fm(n_o2 + p, y2h, y2l, ready=None if p else ("y2_lo", 0))
            pe.wait_ge(sem("acc3"), KD)
            mm(M[0][:, :], ones, acc3[:, :], start=True, stop=True).then_inc(sem("n4_ps"), 1)
            for m in range(KD):
                pe.wait_ge(sem("fo"), m + 1)
                if m >= 3:
                    pe.wait_ge(sem("o_copied"), m - 2)
                for t in range(TT):
                    last = nc.tensor.transpose(M[1 + m % 3][:, t * P:(t + 1) * P], fo[:, m % 2, t * P:(t + 1) * P], ident)
                last.then_inc(sem("o_ps"), 1)

        @block.scalar
        def _(act):
            fn = nc.scalar.activation

            def split(n, with_b=False):
                if n >= N_UNITS:
                    return
                act.wait_ge(sem(f"raw_in{n % 2}"), raw_count(n))
                if n >= 2:
                    act.wait_ge(sem("tile_done"), tiles_before(n - 1))
                s = n % 2
                a = lambda t: t[:, s].rearrange("p k c -> p (k c)")
                if n_b0 <= n < n_c0:
                    fn(a(whi_b), a(raw_b), ACT.Copy)
                fn(a(whi), a(raw), ACT.Copy).then_inc(sem("hi_done"), 1)

            links = [0]

            def link(ins):
                links[0] += 1
                ins.then_inc(sem("act_link"), 1)
                act.wait_ge(sem("act_link"), links[0])

            def rsqrt(dst, mean_of, n):
                link(fn(dst, mean_of, ACT.Ln, scale=1.0 / n, bias=pcol("eps", 0)))
                return fn(dst, dst, ACT.Exp, scale=-0.5)

            def sigmoid(dst, src):
                link(fn(dst, src, ACT.Exp, scale=-1.0))
                link(fn(dst, dst, ACT.Ln, bias=1.0))
                return fn(dst, dst, ACT.Exp, scale=-1.0)

            act.preload_act_table_set(EXP_LN)
            act.wait_ge(sem("par_in"), 16)
            for m in range(KD):
                act.wait_ge(sem("xT_ps"), m + 1)
                fn(hh[:, m, :], (G + M)[m][:, :], ACT.Copy, scale=pcol("g1", m)).then_inc(sem("h_hi"), 1)
            split(0)
            for m in range(4, KD):
                act.wait_ge(sem("h_lo"), m + 1)
                fn(xT[:, m, :], M[m - 4][:, :], ACT.Copy).then_inc(sem("x_kept"), 1)
            split(1)
            for t in range(TT):
                if t >= 1:
                    act.wait_ge(sem("ss"), t)
                fn(sqjunk[:, :], xtm[:, t, :], ACT.Square, accum_out=ss[:, t:t + 1]).then_inc(sem("ss"), 1)
            act.wait_ge(sem("ss"), TT)
            rsqrt(rcol, ss, DM).then_inc(sem("rcol"), 1)
            act.wait_ge(sem("wdt_in"), 16)
            flat = lambda t: t[:, :, :].rearrange("p k c -> p (k c)")
            fn(flat(wdth), flat(wdt), ACT.Copy).then_inc(sem("wdt_hi"), 1)
            fn(ealog, pcol("alog", 0, 4), ACT.Exp).then_inc(sem("ealog"), 1)

            def st_dtT():
                act.wait_ge(sem("dt_abs"), 1)
                fn(dta, dta, ACT.Exp, scale=-1.0).then_inc(sem("dt_exp"), 1)

            def st_cb(g):
                act.wait_ge(sem("cb_ps"), g + 1)
                if g == 1:
                    act.wait_ge(sem("mt"), 2)
                for b, c, a, w in RUNS:
                    last = fn(cbs[:, a:a + w], M[b][:, c:c + w], ACT.Copy)
                last.then_inc(sem("cb_sb"), 1)

            def st_mh1(h):
                act.wait_ge(sem("seg"), h + 1)
                fn(dec[:, :], dec[:, :], ACT.Exp).then_inc(sem("decay"), 1)

            def st_mn(g):
                act.wait_ge(sem("ysum_ps"), g + 1)
                rsqrt(mrs[:, g, :], M[1][:, :], P).then_inc(sem("yrstd"), 1)
                act.wait_ge(sem("yn"), g + 1)
                fn(yh[1][:, g, :], sz[:, g, :], ACT.Copy).then_inc(sem("yc_hi"), 1)

            def st_mo1(h):
                act.wait_ge(sem("mo_nm"), h + 1)
                if h >= 1:
                    act.wait_ge(sem("mo_t"), h)
                for c in range(TT):
                    b, o = QBANK[c]
                    a, w = QREG[c]
                    last = fn(mp[:, a:a + w], M[b][:, o:o + w], ACT.Exp, bias=mnm[:, c:c + 1], accum_out=mls[:, c:c + 1])
                last.then_inc(sem("mo_e"), 1)

            def st_mo2(h):
                act.wait_ge(sem("mo_t"), h + 1)
                if h >= 1:
                    act.wait_ge(sem("mo_o"), h)
                for b, c, a, w in (RUNS[0], RUNS[2]):
                    fn(mpt[:, a:a + w], M[b][:, c:c + w], ACT.Copy).then_inc(sem("mo_pt"), 1)
                for b, c, a, w in (RUNS[1], RUNS[3]):
                    last = fn(mpt[:, a:a + w], M[b][:, c:c + w], ACT.Copy)
                last.then_inc(sem("mo_pt"), 1)

            def out_hi(bank, done, dst, name, h):
                if h % 2:
                    act.wait_ge(sem(done), h + 1)
                    fn(dst[:, h // 2, :], bank[:, :], ACT.Copy).then_inc(sem(name), 1)

            def st_mo3(h):
                out_hi(M[3], "mo_o", ydh, "yd_hi", h)

            def st_st1(h):
                act.wait_ge(sem("st_z"), h + 1)
                if h >= 1:
                    act.wait_ge(sem("st_o"), h)
                for i, (b, c, a, w) in enumerate(RUNS):
                    last = fn(stl[:, a:a + w], M[b][:, c:c + w], ACT.Abs)
                last.then_inc(sem("st_abs"), 1)
                act.wait_ge(sem("st_abs"), h + 1)
                fn(stl[:, :], stl[:, :], ACT.Exp, scale=-1.0).then_inc(sem("st_exp"), 1)
                act.wait_ge(sem("st_exp"), h + 1)
                fn(stl[:, :], stl[:, :], ACT.Ln, bias=1.0).then_inc(sem("st_ln"), 1)

            def st_st2(h):
                act.wait_ge(sem("st_arg"), h + 1)
                fn(stl[:, :], stl[:, :], ACT.Exp).then_inc(sem("st_we"), 1)

            def st_st3(h):
                out_hi(M[3], "st_o", yh[0], "yb_hi", h)

            none = lambda *a: None
            stages = {"dt": none, "dtT": st_dtT, "xsT": none, "acs": none, "cb": st_cb, "mh1": st_mh1, "mh2": none, "mn": st_mn,
                      "mo1": st_mo1, "mo2": st_mo2, "mo3": st_mo3, "st1": st_st1, "st2": st_st2, "st3": st_st3}

            def st_mh2(h):
                if h % 2:
                    act.wait_ge(sem("y_mid"), h // 2 + 1)
                    fn(msq[:, h // 2, :], sz[:, h // 2, :], ACT.Square).then_inc(sem("y_sq"), 1)
            stages["mh2"] = st_mh2

            for n in range(N_A):
                for j in range(2):
                    if j == 0 and n >= 1:
                        split(n + 1)
                    if n in (3, 4, 5):
                        i = 2 * (n - 3) + j
                        if i >= 1:
                            act.wait_ge(sem("silu"), i)
                        if n == 5:
                            act.wait_ge(sem("tile_free"), tiles_before(n) + j + 1)
                            src = sz[:, j, :]
                        else:
                            act.wait_ge(sem("silu_in"), i + 1)
                            src = (xs[:, 0, :], xs[:, 1, :], bm[:, :], cm[:, :])[i]
                        sigmoid(etmp[:, :], src).then_inc(sem("sig"), 1)
                    if n == 2 and j == 1:
                        for f in range(2):
                            act.wait_ge(sem("ya"), f + 1)
                            fn(yh[0][:, f, :], xa[:, f, :], ACT.Copy).then_inc(sem("ya_hi"), 1)
                    run_mix(stages, 2 * n + j)

            for i in range(N_B):
                n = n_b0 + i
                for j in range(2):
                    t = 2 * i + j
                    if j == 0:
                        split(n + 1)
                    act.wait_ge(sem("tile_free"), tiles_before(n) + 2 * j + 1)
                    sigmoid(gt[:, t % 2, :], gt[:, t % 2, :]).then_inc(sem("gate"), 1)
                    if i // 4 == 3:
                        m = t - 24
                        act.wait_ge(sem("m_sum"), m + 1)
                        fn(mh[:, m, :], merged[:, m, :], ACT.Copy).then_inc(sem("m_hi"), 1)
                    run_mix(stages, 24 + t)

            for p in range(4):
                for j in range(2):
                    m = 2 * p + j
                    if j == 0:
                        split(n_c0 + p + 1)
                    act.wait_ge(sem("tile_free"), tiles_before(n_c0) + m + 1)
                    if m >= 2:
                        act.wait_ge(sem("acc0"), m - 1)
                    fn(sq0[:, m % 2, :], xT[:, m, :], ACT.Square).then_inc(sem("sq0"), 1)
                    fn(hh[:, m, :], xT[:, m, :], ACT.Copy, scale=pcol("g2", m)).then_inc(sem("h2_hi"), 1)
            act.wait_ge(sem("n2_ps"), 1)
            rsqrt(R[:, :], M[0][:, :], DM).then_inc(sem("R2"), 1)

            def ffn_unit(n, h, s, nxt):
                nxt()
                act.wait_ge(sem("tile_free"), tiles_before(n) + 1)
                fn(fg_t[:, s, :], fg_t[:, s, :], ACT.Silu).then_inc(sem("gate_act"), 1)

            for f, (n0, part, h0) in enumerate(ffn_units):
                for j in range(part):
                    ffn_unit(n0 + j, h0 + j, (n0 + j) % 2, lambda: split(n0 + j + 1))
                for p in range(4):
                    n = n0 + part + p
                    split(n + 1)
                    if f < 2:
                        continue
                    for j in range(2):
                        m = 2 * p + j
                        act.wait_ge(sem("tile_free"), tiles_before(n) + j + 1)
                        if m >= 2:
                            act.wait_ge(sem("acc2"), m - 1)
                        fn(sq1[:, m % 2, :], xT[:, m, :], ACT.Square)
                        fn(sq2[:, m % 2, :], xT[:, m, :], ACT.Square, scale=pcol("fg", m)).then_inc(sem("sq12"), 1)
                        fn(hh[:, m, :], xT[:, m, :], ACT.Copy, scale=fgng[:, m:m + 1]).then_inc(sem("h3_hi"), 1)
            split(n_e0 + 1)
            act.preload_act_table_set(EXP_LN)
            act.wait_ge(sem("n3_ps"), 1)
            link(fn(r1[:, :], M[0][:, :], ACT.Ln, scale=1.0 / DM, bias=pcol("eps", 0)))
            fn(r2[:, :], r1[:, :], ACT.Exp, scale=-1.0).then_inc(sem("r1_sq"), 1)
            act.wait_ge(sem("r1_sq"), 1)
            fn(r1[:, :], r1[:, :], ACT.Exp, scale=-0.5).then_inc(sem("r1"), 1)
            act.wait_ge(sem("n3_var"), 1)
            rsqrt(r2[:, :], r2[:, :], DM).then_inc(sem("r2"), 1)

            STEPS = KD * TT
            pos = [0]

            def w_exp(s):
                act.wait_ge(sem("w_nm"), s + 1)
                b = 2 * (s % 3)
                c0 = P if s % TT == 0 else 0
                for h in range(2):
                    fn(wp[:, s % 3, h, c0:256], wp[:, s % 3, h, c0:256], ACT.Exp, bias=wnm[:, b + h:b + h + 1],
                       accum_out=wls[:, b + h:b + h + 1])
                fn(wes[:, b:b + 2], wes[:, b:b + 2], ACT.Exp).then_inc(sem("w_e"), 1)

            def w_turned(s):
                act.wait_ge(sem("w_t"), s + 1)
                if s >= 2:
                    act.wait_ge(sem("w_v"), s - 1)
                if s % TT == 0:
                    for h in range(2):
                        last = fn(wpt[:, s % 2, (2 * h + 1) * P:(2 * h + 2) * P], M[2][:, (2 * h + 1) * P:(2 * h + 2) * P], ACT.Copy)
                else:
                    last = fn(wpt[:, s % 2, :], M[2][:, :], ACT.Copy)
                last.then_inc(sem("w_pt"), 1)

            def w_out(s):
                if s % TT == TT - 1:
                    m = s // TT
                    act.wait_ge(sem("w_o"), m + 1)
                    fn(ath[:, m, :], att_t[:, :], ACT.Copy).then_inc(sem("at_hi"), 1)

            def w_slot(limit):
                i = pos[0]
                if 0 <= i - 3 < STEPS:
                    w_out(i - 3)
                if 0 <= i - 2 < STEPS:
                    w_turned(i - 2)
                if i < min(limit, STEPS):
                    w_exp(i)
                    pos[0] += 1
                elif limit == STEPS:
                    pos[0] += 1

            for p in range(4):
                n = n_qz + 2 * p
                lim = 8 * p
                for u in range(2):
                    split(n + u + 1)
                    for j in range(2):
                        w_slot(lim)
                        if u == 1:
                            act.wait_ge(sem("tile_free"), tiles_before(n + 1) + j + 1)
                            if p >= 1:
                                act.wait_ge(sem("za"), 2 * p)
                            sigmoid(za_e[:, j, :], za[:, (2 * p + j) % 4, :]).then_inc(sem("za_e"), 1)
                        w_slot(lim)
            for p in range(4):
                split(n_vs + p + 1)
                for _ in range(4):
                    w_slot(STEPS)
            while pos[0] < STEPS + 3:
                w_slot(STEPS)

            for t in range(TT):
                act.wait_ge(sem("tile_free"), tiles_before(n_vs + 4))
                fn(vg[:, t, :], vg[:, t, :], ACT.Gelu).then_inc(sem("vs_act"), 1)
            act.wait_ge(sem("ln_var"), 1)
            fn(lrs, lrs, ACT.Sqrt).then_inc(sem("ln_rs"), 1)

            def gates(n0, buf, i0, bias0):
                for p in range(4):
                    for u in range(2):
                        split(n0 + 2 * p + u + 1)
                        if u == 0:
                            for j in range(2):
                                m = 2 * p + j
                                act.wait_ge(sem("tile_free"), tiles_before(n0 + 2 * p) + j + 1)
                                fn(buf[:, j, :], buf[:, j, :], ACT.Sigmoid, bias=pcol("bm", bias0 + m)).then_inc(sem("gm_act"), 1)
                        elif i0:
                            for j in range(2):
                                m = 2 * p + j
                                act.wait_ge(sem("y2_sum"), m + 1)
                                fn(y2h[:, m, :], y2[:, m, :], ACT.Copy).then_inc(sem("y2_hi"), 1)

            gates(n_ga, g2t, 0, 0)
            for p in range(4):
                n = n_uz + 2 * p
                split(n + 1)
                for j in range(2):
                    act.wait_ge(sem("tile_free"), tiles_before(n) + j + 1)
                    fn(ub[:, j, :], ub[:, j, :], ACT.Gelu).then_inc(sem("u_act"), 1)
                split(n + 2)
                for j in range(2):
                    act.wait_ge(sem("tile_free"), tiles_before(n + 1) + j + 1)
                    fn(zb[:, j, :], zb[:, j, :], ACT.Silu).then_inc(sem("zs_act"), 1)
                for j in range(2):
                    m = 2 * p + j
                    act.wait_ge(sem("sg"), m + 1)
                    fn(sgh[:, m, :], sgt[:, j, :], ACT.Copy).then_inc(sem("sg_hi"), 1)
            gates(n_gs, g4t, 1, 8)
            for p in range(4):
                split(n_o2 + p + 1)
                for j in range(2):
                    m = 2 * p + j
                    act.wait_ge(sem("tile_free"), tiles_before(n_o2) + m + 1)
                    if m >= 2:
                        act.wait_ge(sem("acc3"), m - 1)
                    fn(sq3[:, m % 2, :], xT[:, m, :], ACT.Square).then_inc(sem("sq3"), 1)
            act.preload_act_table_set(EXP_LN)
            act.wait_ge(sem("n4_ps"), 1)
            rsqrt(R[:, :], M[0][:, :], DM).then_inc(sem("R4"), 1)
            for m in range(KD):
                act.wait_ge(sem("o_ps"), m + 1)
                fn(ot[:, :, m * P:(m + 1) * P], M[1 + m % 3][:, :].rearrange("p (t c) -> p t c", t=TT), ACT.Copy)\
                    .then_inc(sem("o_copied"), 1)

        @block.vector
        def _(dve):
            v = nc.vector
            tt, ts, stt = v.tensor_tensor, v.tensor_scalar, v.scalar_tensor_tensor
            links = [0]

            def link(ins):
                links[0] += 1
                ins.then_inc(sem("dve_link"), 1)
                dve.wait_ge(sem("dve_link"), links[0])

            def tile_ready(T):
                dve.wait_ge(sem("tile_done"), T + 1)

            def scaled(T, dst, scale=None):
                tile_ready(T)
                if scale is None:
                    ins = tt(dst, G[T % 4][:, :], R[:, :], ALU.mult)
                else:
                    ins = stt(out=dst, in0=G[T % 4][:, :], scalar=scale, in1=R[:, :], op0=ALU.mult, op1=ALU.mult)
                ins.then_inc(sem("tile_free"), 1)
                dve.wait_ge(sem("tile_free"), T + 1)

            def scaled_tm(T, dsts, w):
                tile_ready(T)
                for i, (t, dst) in enumerate(dsts):
                    last = ts(dst, G[T % 4][:, i * w:(i + 1) * w], rcol[:, t:t + 1], None, ALU.mult)
                last.then_inc(sem("tile_free"), 1)

            dve.wait_ge(sem("par_in"), 16)
            for m in range(KD):
                dve.wait_ge(sem("h_hi"), m + 1)
                stt(out=hl[:, m, :], in0=(G + M)[m][:, :], scalar=pcol("g1", m), in1=as_f32(hh[:, m, :]),
                    op0=ALU.mult, op1=ALU.subtract).then_inc(sem("h_lo"), 1)
            for m in range(4):
                v.tensor_copy(xT[:, m, :], G[m][:, :]).then_inc(sem("xg_kept"), 1)
            tt(fgng, pcol("fg", 0, 8), pcol("ng2", 0, 8), ALU.mult)
            dve.wait_ge(sem("rcol"), 1)
            for t in range(TT):
                last = ts(xbuf[:, t, 0:P], ident, rcol[:, t:t + 1], None, ALU.mult)
            last.then_inc(sem("rdiag"), 1)
            dve.wait_ge(sem("r_ps"), 1)
            link(v.tensor_copy(R[:, :], M[0][:, :]))
            v.memset(cbuf[:, :, 0:2], 0.0)
            link(v.memset(xbuf[:, :, 0:3], 0.0))
            dve.wait_ge(sem("wdt_hi"), 1)
            flat = lambda t: t[:, :, :].rearrange("p k c -> p (k c)")
            tt(flat(wdtl), flat(wdt), as_f32(flat(wdth)), ALU.subtract).then_inc(sem("wdt_lo"), 1)

            def conv_a(f):
                link(tt(cbuf[:, f, 2:], cbuf[:, f, 2:], xa[:, f, :], ALU.mult))
                link(ts(xa[:, f, :], cbuf[:, f, 0:SEQ], pcol("ca", f), None, ALU.mult))
                for k in (1, 2):
                    link(stt(out=xa[:, f, :], in0=cbuf[:, f, k:k + SEQ], scalar=pcol("ca", 2 * k + f), in1=xa[:, f, :],
                             op0=ALU.mult, op1=ALU.add))
                tt(xa[:, f, :], xa[:, f, :], bgate[:, f, :], ALU.mult).then_inc(sem("ya"), 1)

            def silu_out(i, dst, val):
                dve.wait_ge(sem("sig"), i + 1)
                tt(dst, val, etmp[:, :], ALU.mult).then_inc(sem("silu"), 1)

            conv_dst = [xs[:, 0, :], xs[:, 1, :], bm[:, :], cm[:, :]]

            def conv_c(f):
                d = conv_dst[f]
                link(ts(d, xbuf[:, f, 0:SEQ], pcol("cw", f), pcol("cb", f), ALU.mult, ALU.add))
                for k in (1, 2, 3):
                    last = stt(out=d, in0=xbuf[:, f, k:k + SEQ], scalar=pcol("cw", 4 * k + f), in1=d, op0=ALU.mult, op1=ALU.add)
                    if k < 3:
                        link(last)
                last.then_inc(sem("silu_in"), 1)
                silu_out(f, d, d)

            def st_dt():
                dve.wait_ge(sem("dt_ps"), 1)
                tt(dtf[:, :], M[0][0:HEADS, :], R[0:HEADS, :], ALU.mult).then_inc(sem("dt_f"), 1)

            def st_dtT():
                dve.wait_ge(sem("dtT_ps"), 1)
                for t in range(TT):
                    a = slice(t * HEADS, (t + 1) * HEADS)
                    last = tt(dtv[:, a], M[0][:, a], pcol("dtb", 0, 4), ALU.add)
                last.then_inc(sem("dtv_read"), 1)
                dve.wait_ge(sem("dtv_read"), 1)
                link(ts(dts, dtv, -1.0, None, ALU.mult))
                tt(dta, dtv, dts, ALU.max).then_inc(sem("dt_abs"), 1)
                dve.wait_ge(sem("dt_exp"), 1)
                link(ts(dts, dta, 2.0, None, ALU.add))
                link(v.reciprocal(dts, dts))
                link(tt(dts, dta, dts, ALU.mult))
                link(tt(dts2, dts, dts, ALU.mult))
                link(ts(dtq, dts2, 1.0 / 17, None, ALU.mult))
                for d in (15, 13, 11, 9, 7, 5, 3):
                    link(stt(out=dtq, in0=dtq, scalar=1.0 / d, in1=dts2, op0=ALU.add, op1=ALU.mult))
                link(stt(out=dtq, in0=dtq, scalar=1.0, in1=dts, op0=ALU.add, op1=ALU.mult))
                link(ts(dtv, dtv, 0.0, None, ALU.max))
                link(stt(out=dtv, in0=dtq, scalar=2.0, in1=dtv, op0=ALU.mult, op1=ALU.add))
                dve.wait_ge(sem("ealog"), 1)
                stt(out=adt.rearrange("p (t h) -> p t h", h=HEADS), in0=dtv.rearrange("p (t h) -> p t h", h=HEADS), scalar=-1.0,
                    in1=ealog.unsqueeze(1).broadcast_to((P, TT, HEADS)), op0=ALU.mult, op1=ALU.mult).then_inc(sem("adt"), 1)

            def spread(h):
                dve.wait_ge(sem("adt"), 1)
                if h >= 1:
                    dve.wait_ge(sem("acsb_ps"), h)
                a = adt.rearrange("p (t h) -> p t h", h=HEADS)[:, :, h:h + 1]
                v.tensor_copy(adtb[:, :, :], a.broadcast_to((P, TT, P))).then_inc(sem("adtb"), 1)

            def st_xsT():
                for b in range(2):
                    dve.wait_ge(sem("xsT_ps"), b + 1)
                    for i in range(2):
                        t = 2 * b + i
                        d = dtv[:, t * HEADS:(t + 1) * HEADS].unsqueeze(2).broadcast_to((P, HEADS, DH))
                        last = tt(xdt[:, t, :].rearrange("p (h d) -> p h d", h=HEADS),
                                  M[1 + b][:, i * BW:(i + 1) * BW].rearrange("p (h d) -> p h d", h=HEADS), d, ALU.mult)
                    last.then_inc(sem("xdt"), 1)

            def st_acs():
                dve.wait_ge(sem("acs_ps"), 1)
                v.tensor_copy(acs, M[3][:, 0:16]).then_inc(sem("acs"), 1)
                spread(0)

            def st_cb(g):
                dve.wait_ge(sem("cb_sb"), g + 1)
                for a, _ in REG:
                    last = tt(cbs[:, a:a + P], cbs[:, a:a + P], u_incl, ALU.mult)
                last.then_inc(sem("cbs"), 1)

            def st_mh1(h):
                dve.wait_ge(sem("acsb_ps"), h + 1)
                if h >= 1:
                    dve.wait_ge(sem("y_ps"), h)
                else:
                    dve.wait_ge(sem("acs"), 1)
                for n, (a, w) in enumerate(REG):
                    last = ts(dec[:, a:a + w], M[3][:, n * P:SEQ], acs[:, n * HEADS + h:n * HEADS + h + 1], 0.0,
                              ALU.subtract, ALU.min)
                last.then_inc(sem("seg"), 1)
                if h + 1 < HEADS:
                    spread(h + 1)
                dve.wait_ge(sem("decay"), h + 1)
                dve.wait_ge(sem("cbs"), h // 2 + 1)
                tt(dec[:, :], dec[:, :], cbs[:, :], ALU.mult).then_inc(sem("mt"), 1)

            def st_mh2(h):
                if h % 2 == 0:
                    return
                f = h // 2
                dve.wait_ge(sem("y_ps"), h + 1)
                link(stt(out=xs[:, f, :], in0=xs[:, f, :], scalar=pcol("dsk", f), in1=M[0][:, :], op0=ALU.mult, op1=ALU.add))
                tt(sz[:, f, :], xs[:, f, :], sz[:, f, :], ALU.mult).then_inc(sem("y_mid"), 1)

            def st_mn(g):
                dve.wait_ge(sem("yrstd"), g + 1)
                stt(out=sz[:, g, :], in0=sz[:, g, :], scalar=pcol("ng", g), in1=mrs[:, g, :], op0=ALU.mult, op1=ALU.mult)\
                    .then_inc(sem("yn"), 1)
                dve.wait_ge(sem("yc_hi"), g + 1)
                tt(yl[1][:, g, :], sz[:, g, :], as_f32(yh[1][:, g, :]), ALU.subtract).then_inc(sem("yc_lo"), 1)

            def st_mo1(h):
                dve.wait_ge(sem("mo_s"), h + 1)
                for c in range(TT):
                    b, o = QBANK[c]
                    last = v.reduce_max(mmx[:, c:c + 1], M[b][:, o:o + (c + 1) * P], AX.X)
                link(last)
                if h >= 1:
                    dve.wait_ge(sem("mo_e"), h)
                ts(mnm, mmx, -1.0, None, ALU.mult).then_inc(sem("mo_nm"), 1)
                dve.wait_ge(sem("mo_e"), h + 1)
                link(v.reciprocal(mrl, mls))
                for c in range(TT):
                    a, w = QREG[c]
                    last = ts(mp[:, a:a + w], mp[:, a:a + w], mrl[:, c:c + 1], None, ALU.mult)
                last.then_inc(sem("mo_p"), 1)

            def out_lo(hi_name, dst_h, dst_l, name, h):
                if h % 2:
                    f = h // 2
                    dve.wait_ge(sem(hi_name), f + 1)
                    tt(dst_l[:, f, :], M[3][:, :], as_f32(dst_h[:, f, :]), ALU.subtract).then_inc(sem(name), 1)

            def st_mo3(h):
                out_lo("yd_hi", ydh, ydl, "yd_lo", h)

            def st_st1(h):
                dve.wait_ge(sem("st_ln"), h + 1)
                if h >= 1:
                    dve.wait_ge(sem("st_b"), h)
                for b, c, a, w in RUNS:
                    last = stt(out=stsp[:, a:a + w], in0=M[b][:, c:c + w], scalar=0.0, in1=stl[:, a:a + w], op0=ALU.max, op1=ALU.add)
                link(last)
                for b, c, a, w in RUNS:
                    stt(out=stl[:, a:a + w], in0=M[b][:, c:c + w], scalar=0.0, in1=stl[:, a:a + w], op0=ALU.min, op1=ALU.subtract)
                for a, _ in REG:
                    last = tt(stsp[:, a:a + P], stsp[:, a:a + P], u_strict, ALU.mult)
                last.then_inc(sem("st_sp"), 1)

            def st_st2(h):
                dve.wait_ge(sem("st_b"), h + 1)
                dve.wait_ge(sem("st_sp"), h + 1)
                for b, c, a, w in RUNS:
                    last = tt(stl[:, a:a + w], stl[:, a:a + w], M[b][:, c:c + w], ALU.subtract)
                last.then_inc(sem("st_arg"), 1)
                dve.wait_ge(sem("st_we"), h + 1)
                for a, _ in REG:
                    last = tt(stl[:, a:a + P], stl[:, a:a + P], u_strict, ALU.mult)
                last.then_inc(sem("st_w"), 1)

            def st_st3(h):
                out_lo("yb_hi", yh[0], yl[0], "yb_lo", h)

            none = lambda *a: None
            stages = {"dt": st_dt, "dtT": st_dtT, "xsT": st_xsT, "acs": st_acs, "cb": st_cb, "mh1": st_mh1, "mh2": st_mh2, "mn": st_mn,
                      "mo1": st_mo1, "mo2": none, "mo3": st_mo3, "st1": st_st1, "st2": st_st2, "st3": st_st3}

            for n in range(N_A):
                for j in range(2):
                    T = tiles_before(n) + j
                    if n == 0:
                        scaled(T, xa[:, j, :])
                    elif n == 1:
                        scaled(T, bgate[:, j, :])
                    elif n == 2:
                        scaled(T, cbuf[:, j, 2:])
                        if j == 1:
                            for f in range(2):
                                conv_a(f)
                            for f in range(2):
                                dve.wait_ge(sem("ya_hi"), f + 1)
                                tt(yl[0][:, f, :], xa[:, f, :], as_f32(yh[0][:, f, :]), ALU.subtract).then_inc(sem("ya_lo"), 1)
                    elif n in (3, 4):
                        f = 2 * (n - 3) + j
                        scaled(T, xbuf[:, f, 3:])
                        conv_c(f)
                    elif n == 5:
                        scaled(T, sz[:, j, :])
                        silu_out(4 + j, sz[:, j, :], sz[:, j, :])
                    elif n in (6, 9):
                        scaled(T, (qd if n == 6 else qb)[:, j, :], DH ** -0.5)
                    elif n in (7, 10):
                        scaled(T, (kd if n == 7 else kb)[:, j, :])
                    else:
                        d = vd if n == 8 else vb
                        scaled_tm(T, [(2 * j + i, d[:, 2 * j + i, :]) for i in range(2)], BW)
                    run_mix(stages, 2 * n + j)

            for i in range(N_B):
                n, br = n_b0 + i, i // 4
                for j in range(2):
                    t, T = 2 * i + j, tiles_before(n_b0 + i) + 2 * j
                    m, g = t % KD, gt[:, t % 2, :]
                    tile_ready(T)
                    tt(g, G[T % 4][:, :], R[:, :], ALU.mult).then_inc(sem("tile_free"), 1)
                    dve.wait_ge(sem("gate"), t + 1)
                    tile_ready(T + 1)
                    if br == 0:
                        tt(merged[:, m, :], G[(T + 1) % 4][:, :], g, ALU.mult).then_inc(sem("tile_free"), 1)
                    else:
                        tt(g, G[(T + 1) % 4][:, :], g, ALU.mult).then_inc(sem("tile_free"), 1)
                        dve.wait_ge(sem("tile_free"), T + 2)
                        last = tt(merged[:, m, :], merged[:, m, :], g, ALU.add)
                        if br == 3:
                            last.then_inc(sem("m_sum"), 1)
                            for mm_ in ([m - 1] if m else []) + ([m] if m == KD - 1 else []):
                                dve.wait_ge(sem("m_hi"), mm_ + 1)
                                tt(ml[:, mm_, :], merged[:, mm_, :], as_f32(mh[:, mm_, :]), ALU.subtract).then_inc(sem("m_lo"), 1)
                        else:
                            link(last)
                    run_mix(stages, 24 + t)

            def accumulate(acc, sq, m, name):
                if m == 0:
                    v.tensor_copy(acc[:, :], sq[:, 0, :]).then_inc(sem(name), 1)
                else:
                    dve.wait_ge(sem(name), m)
                    tt(acc[:, :], acc[:, :], sq[:, m % 2, :], ALU.add).then_inc(sem(name), 1)

            def add_residual(T, m):
                tile_ready(T)
                tt(xT[:, m, :], xT[:, m, :], G[T % 4][:, :], ALU.add).then_inc(sem("tile_free"), 1)

            for m in range(KD):
                add_residual(tiles_before(n_c0) + m, m)
                dve.wait_ge(sem("sq0"), m + 1)
                accumulate(acc0, sq0, m, "acc0")
                dve.wait_ge(sem("h2_hi"), m + 1)
                stt(out=hl[:, m, :], in0=xT[:, m, :], scalar=pcol("g2", m), in1=as_f32(hh[:, m, :]),
                    op0=ALU.mult, op1=ALU.subtract).then_inc(sem("h2_lo"), 1)
            dve.wait_ge(sem("R2"), 1)

            for f, (n0, part, h0) in enumerate(ffn_units):
                for j in range(part):
                    n, h, T = n0 + j, h0 + j, tiles_before(n0 + j)
                    s = n % 2
                    tile_ready(T)
                    tt(fg_t[:, s, :], G[T % 4][:, :], R[:, :], ALU.mult).then_inc(sem("tile_free"), 1)
                    scaled(T + 1, fu_t[:, s, :])
                    dve.wait_ge(sem("gate_act"), h + 1)
                    link(tt(fu_t[:, s, :], fu_t[:, s, :], fg_t[:, s, :], ALU.mult))
                    link(v.tensor_copy(ah[:, j, :], fu_t[:, s, :]))
                    tt(al[:, j, :], fu_t[:, s, :], as_f32(ah[:, j, :]), ALU.subtract).then_inc(sem("act_lo"), 1)
                for m in range(KD):
                    T = tiles_before(n0 + part) + m
                    add_residual(T, m)
                    if f == 2:
                        dve.wait_ge(sem("sq12"), m + 1)
                        accumulate(acc1, sq1, m, "acc1")
                        accumulate(acc2, sq2, m, "acc2")
                        dve.wait_ge(sem("h3_hi"), m + 1)
                        stt(out=hl[:, m, :], in0=xT[:, m, :], scalar=fgng[:, m:m + 1], in1=as_f32(hh[:, m, :]),
                            op0=ALU.mult, op1=ALU.subtract).then_inc(sem("h3_lo"), 1)
                    else:
                        dve.wait_ge(sem("tile_free"), T + 1)

            dve.wait_ge(sem("r1_sq"), 1)
            tt(r2[:, :], M[1][:, :], r2[:, :], ALU.mult).then_inc(sem("n3_var"), 1)
            dve.wait_ge(sem("r1"), 1)
            dve.wait_ge(sem("r2"), 1)
            tt(R[:, :], r1[:, :], r2[:, :], ALU.mult).then_inc(sem("R3"), 1)

            T = tiles_before(n_e0)
            dve.wait_ge(sem("c2_in"), 80)
            tile_ready(T)
            dve.wait_ge(sem("R3"), 1)
            tt(rope_q[:, 0, :], G[T % 4][:, :], R[:, :], ALU.mult).then_inc(sem("tile_free"), 1)
            for m in range(KD):
                last = stt(out=xT[:, m, :], in0=xT[:, m, :], scalar=pcol("fg", m), in1=r1[:, :], op0=ALU.mult, op1=ALU.mult)
            link(last)
            dve.wait_ge(sem("rcol_ps"), 1)
            link(v.tensor_copy(rcol, M[2][:, :].rearrange("p (t c) -> p t c", t=TT)[:, :, 0]))
            tile_ready(T + 1)
            for t in range(TT):
                last = ts(v2[:, t, :], G[(T + 1) % 4][:, t * P:(t + 1) * P], rcol[:, t:t + 1], None, ALU.mult)
            last.then_inc(sem("tile_free"), 1)
            dve.wait_ge(sem("wT_ps"), 1)
            for b in range(2):
                last = v.tensor_copy(wT[:, 4 * b:4 * b + 4, :].rearrange("p g i -> p (g i)"), M[b][:, :])
            last.then_inc(sem("wT_read"), 1)
            dve.wait_ge(sem("wT_read"), 1)
            v.memset(wT[64:P, :, 0:64], 0.0).then_inc(sem("wT_ready"), 1)

            def rope(i, j, bank):
                dve.wait_ge(sem("rope_ps"), i + 1)
                tt(rope_t[:, j, :], bank[:, :], cs2[:, 1, :], ALU.mult)
                link(tt(rope_q[:, j, :], rope_q[:, j, :], cs2[:, 0, :], ALU.mult))

            def finish_keys():
                rope(0, 0, M[3])
                for kv in range(2):
                    for half in range(2):
                        r = slice(64 * kv, 64 * kv + 64)
                        last = tt(k2[64 * half:64 * half + 64, kv, :], rope_q[r, 0, :], rope_t[r, 0, :], ALU.add)
                last.then_inc(sem("k_ready"), 1)
                dve.wait_ge(sem("k_ready"), 1)

            STEPS = KD * TT
            pos = [0]
            mask = perm[:, P:P + 256]

            def w_soft(s):
                m, c = s // TT, s % TT
                b, sl = 2 * (s % 3), s % 3
                c0 = P if c == 0 else 0
                dve.wait_ge(sem("w_ps"), s + 1)
                if s >= 3:
                    dve.wait_ge(sem("w_t"), s - 2)
                for h in range(2):
                    last = tt(wp[:, sl, h, c0:256], M[h][:, c0:256], mask[:, c0:256], ALU.add)
                last.then_inc(sem("w_s"), 1)
                dve.wait_ge(sem("w_s"), s + 1)
                link(v.reduce_max(wmx[:, b:b + 2], wp[:, sl, :, c0:256], AX.X))
                link(tt(wmx[:, b:b + 2], wmx[:, b:b + 2], pcol("sink", 2 * m, 2), ALU.max))
                link(ts(wnm[:, b:b + 2], wmx[:, b:b + 2], -1.0, None, ALU.mult))
                tt(wes[:, b:b + 2], wnm[:, b:b + 2], pcol("sink", 2 * m, 2), ALU.add).then_inc(sem("w_nm"), 1)

            def w_norm(s):
                b, sl = 2 * (s % 3), s % 3
                c0 = P if s % TT == 0 else 0
                dve.wait_ge(sem("w_e"), s + 1)
                link(tt(wls[:, b:b + 2], wls[:, b:b + 2], wes[:, b:b + 2], ALU.add))
                link(v.reciprocal(wls[:, b:b + 2], wls[:, b:b + 2]))
                for h in range(2):
                    last = ts(wp[:, sl, h, c0:256], wp[:, sl, h, c0:256], wls[:, b + h:b + h + 1], None, ALU.mult)
                last.then_inc(sem("w_p"), 1)

            def w_out(s):
                if s % TT == TT - 1:
                    m = s // TT
                    dve.wait_ge(sem("w_v"), s + 1)
                    tt(att_t[:, :], M[3][:, :], za[:, m % 4, :], ALU.mult).then_inc(sem("w_o"), 1)

            def w_rest(s):
                if s % TT == TT - 1:
                    m = s // TT
                    dve.wait_ge(sem("at_hi"), m + 1)
                    tt(atl[:, m, :], att_t[:, :], as_f32(ath[:, m, :]), ALU.subtract).then_inc(sem("at_lo"), 1)

            def w_slot(limit):
                i = pos[0]
                if i >= limit and limit < STEPS:
                    return
                if 0 <= i - 1 < STEPS:
                    w_norm(i - 1)
                if 0 <= i - 4 < STEPS:
                    w_rest(i - 4)
                if 0 <= i - 3 < STEPS:
                    w_out(i - 3)
                if i < STEPS:
                    w_soft(i)
                pos[0] += 1

            for p in range(4):
                n = n_qz + 2 * p
                lim = 8 * p
                for u in range(2):
                    for j in range(2):
                        m, T = 2 * p + j, tiles_before(n + u) + j
                        w_slot(lim)
                        if u == 1 and j == 0:
                            for i in range(2):
                                rope(1 + 2 * p + i, i, G[(tiles_before(n) + i) % 4])
                                tt(q2[:, (2 * p + i) % 4, :], rope_q[:, i, :], rope_t[:, i, :], ALU.add).then_inc(sem("tile_free"), 1)
                        tile_ready(T)
                        if u == 0:
                            if p == 0 and j == 0:
                                finish_keys()
                            stt(out=rope_q[:, j, :], in0=G[T % 4][:, :], scalar=DH ** -0.5, in1=R[:, :], op0=ALU.mult, op1=ALU.mult)\
                                .then_inc(sem("rope_in"), 1)
                        else:
                            scaled(T, za[:, m % 4, :])
                        w_slot(lim)
                for j in range(2):
                    m = 2 * p + j
                    dve.wait_ge(sem("za_e"), m + 1)
                    last = tt(za[:, m % 4, :], za[:, m % 4, :], za_e[:, j, :], ALU.mult)
                    last.then_inc(sem("za"), 1)
                dve.wait_ge(sem("za"), 2 * p + 2)
            for p in range(4):
                n = n_vs + p
                for j in range(2):
                    T = tiles_before(n) + j
                    w_slot(STEPS)
                    w_slot(STEPS)
                    tile_ready(T)
                    for i in range(2):
                        t = (T % 2) * 2 + i
                        last = ts(vg[:, t, p * UC:(p + 1) * UC], G[T % 4][:, i * UC:(i + 1) * UC], rcol[:, t:t + 1], None, ALU.mult)
                    last.then_inc(sem("tile_free"), 1)
                    dve.wait_ge(sem("tile_free"), T + 1)
            while pos[0] < STEPS + 4:
                w_slot(STEPS)

            for t in range(TT):
                dve.wait_ge(sem("vs_act"), t + 1)
                for half in range(2):
                    last = v.bn_stats(bns[:, (2 * t + half) * 6:(2 * t + half + 1) * 6], vg[:, t, half * 512:(half + 1) * 512])
            link(last)
            for t in range(TT):
                last = v.bn_aggr(mv[:, 2 * t:2 * t + 2], bns[:, 12 * t:12 * t + 12])
            link(last)
            link(ts(lrs, mv.rearrange("p (t a) -> p t a", a=2)[:, :, 1], EPS, None, ALU.add))
            v.reciprocal(lrs, lrs).then_inc(sem("ln_var"), 1)
            dve.wait_ge(sem("ln_rs"), 1)

            def layer_norm(t):
                link(ts(vg[:, t, :], vg[:, t, :], mv[:, 2 * t:2 * t + 1], lrs[:, t:t + 1], ALU.subtract, ALU.mult))
                link(tt(vg[:, t, :], vg[:, t, :], lng[:, :], ALU.mult))
                tt(vg[:, t, :], vg[:, t, :], lnb[:, :], ALU.add).then_inc(sem("vb_ready"), 1)

            def gates(n0, buf, second):
                for p in range(4):
                    n = n0 + 2 * p
                    for j in range(2):
                        scaled(tiles_before(n) + j, buf[:, j, :])
                    if not second:
                        layer_norm(p)
                    for j in range(2):
                        m, T = 2 * p + j, tiles_before(n + 1) + j
                        dve.wait_ge(sem("gm_act"), m + 1 + (KD if second else 0))
                        tile_ready(T)
                        if not second:
                            tt(y2[:, m, :], G[T % 4][:, :], buf[:, j, :], ALU.mult).then_inc(sem("tile_free"), 1)
                            dve.wait_ge(sem("tile_free"), T + 1)
                        else:
                            tt(buf[:, j, :], G[T % 4][:, :], buf[:, j, :], ALU.mult).then_inc(sem("tile_free"), 1)
                            dve.wait_ge(sem("tile_free"), T + 1)
                            tt(y2[:, m, :], y2[:, m, :], buf[:, j, :], ALU.add).then_inc(sem("y2_sum"), 1)
                            dve.wait_ge(sem("y2_hi"), m + 1)
                            tt(y2l[:, m, :], y2[:, m, :], as_f32(y2h[:, m, :]), ALU.subtract).then_inc(sem("y2_lo"), 1)

            gates(n_ga, g2t, False)
            for p in range(4):
                n = n_uz + 2 * p
                for j in range(2):
                    scaled(tiles_before(n) + j, ub[:, j, :])
                for j in range(2):
                    scaled(tiles_before(n + 1) + j, zb[:, j, :])
                for j in range(2):
                    m = 2 * p + j
                    dve.wait_ge(sem("mixed_ps"), m + 1)
                    d = sgt[:, j, :]
                    ins = tt(d.rearrange("p (t i) -> p t i", t=TT), M[m % 2][:, :].rearrange("p (t i) -> p t i", t=TT),
                             bsb[:, m, :].unsqueeze(1).broadcast_to((P, TT, P)), ALU.add)
                    ins.then_inc(sem("mixed"), 1)
                    dve.wait_ge(sem("mixed"), m + 1)
                    dve.wait_ge(sem("u_act"), m + 1)
                    link(tt(d, d, ub[:, j, :], ALU.mult))
                    dve.wait_ge(sem("zs_act"), m + 1)
                    tt(d, d, zb[:, j, :], ALU.mult).then_inc(sem("sg"), 1)
                    dve.wait_ge(sem("sg_hi"), m + 1)
                    tt(sgl[:, m, :], d, as_f32(sgh[:, m, :]), ALU.subtract).then_inc(sem("sg_lo"), 1)
            gates(n_gs, g4t, True)

            for m in range(KD):
                add_residual(tiles_before(n_o2) + m, m)
                dve.wait_ge(sem("sq3"), m + 1)
                accumulate(acc3, sq3, m, "acc3")
            dve.wait_ge(sem("R4"), 1)
            for m in range(KD):
                if m >= 2:
                    dve.wait_ge(sem("o_ps"), m - 1)
                stt(out=fo[:, m % 2, :], in0=xT[:, m, :], scalar=pcol("fg2", m), in1=R[:, :], op0=ALU.mult, op1=ALU.mult)\
                    .then_inc(sem("fo"), 1)


def constants():
    i = np.arange(P)
    f = np.float32
    upper = np.concatenate([(i[:, None] <= i[None, :]).astype(f), np.ones((P, 3 * P), f)], 1)
    cst1 = np.concatenate([np.eye(P, dtype=f), upper, (i[:, None] < i[None, :]).astype(f),
                           (i[:, None] > i[None, :]).astype(f),
                           np.where(i[None, :] > i[:, None], f(NEG), f(0)).astype(f)], 1)
    half = 8
    inv = f(500000.0) ** (-(np.arange(half, dtype=f) * f(2.0)) / f(16))
    ang = np.arange(SEQ, dtype=f)[None, :] * inv[:, None].astype(f)
    cos, sin = np.ones((64, SEQ), f), np.zeros((64, SEQ), f)
    cos[0:8] = cos[8:16] = np.cos(ang)
    sin[0:8], sin[8:16] = -np.sin(ang), np.sin(ang)
    swap = np.zeros((P, P), f)
    for h in range(2):
        for d in range(half):
            swap[64 * h + d + half, 64 * h + d] = swap[64 * h + d, 64 * h + d + half] = 1
    win = np.zeros((P, 256), f)
    win[0:64, 192:256] = NEG
    win[64:128, 0:64] = NEG
    cst2a = np.concatenate([np.tile(cos, (2, 1)), np.tile(sin, (2, 1))], 1)
    return cst1, cst2a, np.concatenate([swap, win], 1)


def kernel(x, norm1_g, w_in, conv_a_w, ssm_conv_w, ssm_conv_b, ssm_dt_bias, ssm_a_log, ssm_d, ssm_norm_g, w_branch,
           w_o, norm2_g, w_gate_up, w_down, final_g, norm_g_2, w_in_2, b_merge_2, att_sinks_2, sg_w_2, sg_b_2,
           sg_ln_g_2, sg_ln_b_2, w_att_out_2, w_sg_out_2, w_o_2, final_g_2):
    import concourse.bacc as bacc
    from concourse.bass_utils import run_bass_kernel_spmd

    col = lambda a: np.asarray(a).reshape(-1, P).T
    row = lambda a: np.broadcast_to(np.asarray(a).reshape(1, -1), (P, np.asarray(a).size))
    par = np.ascontiguousarray(np.concatenate([
        col(norm1_g), col(conv_a_w), col(ssm_conv_w), col(ssm_conv_b), col(ssm_norm_g),
        np.repeat(np.asarray(ssm_d).reshape(2, 2).T, 64, axis=0), col(norm2_g), col(final_g), col(norm_g_2), col(b_merge_2),
        col(final_g_2), row(att_sinks_2), row(ssm_dt_bias), row(ssm_a_log),
        np.full((P, 1), EPS, np.float32)], axis=1))
    cst1, cst2a, cst2b = constants()
    a = np.asarray
    arrays = {
        "x": a(x)[0], "par": par, "cst1": cst1, "cst2a": cst2a, "cst2b": cst2b, "w_in": a(w_in)[0], "w_branch": a(w_branch)[0],
        "w_o": a(w_o)[0], "w_gu": a(w_gate_up)[0], "w_down": a(w_down)[0], "w_in2": a(w_in_2)[0], "sg_w": a(sg_w_2)[0],
        "sg_b": a(sg_b_2).reshape(-1), "ln_g": a(sg_ln_g_2).reshape(-1), "ln_b": a(sg_ln_b_2).reshape(-1),
        "w_ao": a(w_att_out_2)[0], "w_so": a(w_sg_out_2)[0], "w_o2": a(w_o_2)[0],
    }
    arrays = {k: np.ascontiguousarray(v) for k, v in arrays.items()}
    nc = bacc.Bacc("TRN2", target_bir_lowering=False, num_devices=1)
    ins = [nc.dram_tensor(k, v.shape, mybir.dt.from_np(v.dtype), kind="ExternalInput").ap() for k, v in arrays.items()]
    out = nc.dram_tensor("out", (SEQ, DM), mybir.dt.float32, kind="ExternalOutput").ap()
    build_program(nc, *ins, out)
    r = run_bass_kernel_spmd(nc, [arrays], core_ids=[0])
    return np.asarray(r.results[0]["out"]).reshape(1, SEQ, DM)
```

```python
import numpy as np
import concourse.bass as bass
from concourse import mybir
from contextlib import ExitStack

SEQ, DM = 512, 1024
P = 128
KD = DM // P
TT = SEQ // P
HEADS, DH = 4, 64
BW = HEADS * DH
FFN = 2816
FFN_PARTS = (8, 8, 6)
EPS = 1e-6
NEG = -1e30
UC = 256
KB = 1024

IN_XA, IN_BG, IN_CG = 0, BW, 2 * BW
IN_QB, IN_KB, IN_VB = 3 * BW, 4 * BW, 5 * BW
IN_Z, IN_X, IN_BC, IN_DT = 6 * BW, 7 * BW, 8 * BW, 9 * BW
IN_QD = IN_DT + HEADS
IN_KD, IN_VD = IN_QD + BW, IN_QD + 2 * BW
IN_G = IN_QD + 3 * BW
AH, GW = 16, 128
I2_Q, I2_K, I2_V, I2_ZA = 0, 1024, 1152, 1280
I2_U, I2_VS, I2_ZS, I2_GA, I2_GS = 2304, 3328, 4352, 5376, 6400

PAR = {}
_at = 0
for _n, _w in (("g1", 8), ("ca", 6), ("cw", 16), ("cb", 4), ("ng", 2), ("dsk", 2), ("g2", 8), ("fg", 8),
               ("ng2", 8), ("bm", 16), ("fg2", 8), ("sink", 16), ("dtb", 4), ("alog", 4),
               ("eps", 1)):
    PAR[_n] = (_at, _w)
    _at += _w
NPAR = _at

REG = [(0, 512), (512, 384), (896, 256), (1152, 128)]
RBANK = [(0, 0), (1, 0), (2, 0), (1, 384)]
QREG = [(1152, 128), (896, 256), (512, 384), (0, 512)]
QBANK = [(1, 384), (2, 0), (1, 0), (0, 0)]
RUNS = [(0, 0, 0, 512), (1, 0, 512, 384), (2, 0, 896, 256), (1, 384, 1152, 128)]


def build_program(nc, x, par, cst1, cst2a, cst2b, w_in, w_branch, w_o, w_gu, w_down, w_in2, sg_w, sg_b, ln_g,
                  ln_b, w_ao, w_so, w_o2, out):
    f32, f32r = mybir.dt.float32, mybir.dt.float32r
    ALU, ACT = mybir.AluOpType, mybir.ActivationFunctionType
    AX = mybir.AxisListType
    EXP_LN, EXP_TANH = "natural_log_exp_and_others", "exp_and_others"

    ctx = ExitStack()
    with ctx:
        base = (nc.sbuf_base + 31) // 32 * 32

        def place(name, shape, kb, dt=f32):
            return nc.alloc_sbuf_tensor_at(name, shape, dt, offset=base + int(kb * KB))

        sems = {}

        def sem(name):
            if name not in sems:
                sems[name] = ctx.enter_context(nc.semaphore(name))
            return sems[name]

        raw = place("raw", [P, 2, 8, UC], 0)
        whi = place("whi", [P, 2, 8, UC], 16, f32r)
        wlo = place("wlo", [P, 2, 8, UC], 32, f32r)
        raw_b = place("raw_b", [P, 2, 2, UC], 48)
        whi_b = place("whi_b", [P, 2, 2, UC], 52, f32r)
        wlo_b = place("wlo_b", [P, 2, 2, UC], 56, f32r)
        xT = place("xT", [P, KD, SEQ], 60)
        hh = place("hh", [P, KD, SEQ], 76, f32r)
        hl = place("hl", [P, KD, SEQ], 92, f32r)
        c1 = place("c1", [P, 1024], 108)
        prm = place("prm", [P, NPAR], 112)
        sml = place("sml", [P, 256], 113)
        R = place("R", [P, SEQ], 114)
        Z0 = 116.0
        xtm = place("xtm", [P, TT, DM], Z0)
        xa = place("xa", [P, 2, SEQ], Z0)
        bgate = place("bgate", [P, 2, SEQ], Z0 + 4)
        cbuf = place("cbuf", [P, 2, SEQ + 2], Z0 + 8)
        merged = place("merged", [P, KD, SEQ], Z0)
        yh = [place(f"yh{i}", [P, 2, SEQ], Z0 + 16 + 8 * i, f32r) for i in range(2)]
        yl = [place(f"yl{i}", [P, 2, SEQ], Z0 + 20 + 8 * i, f32r) for i in range(2)]
        U0 = Z0 + 32
        mh = place("mh", [P, KD, SEQ], U0, f32r)
        ml = place("ml", [P, KD, SEQ], U0 + 16, f32r)
        xs = place("xs", [P, 2, SEQ], U0)
        bm = place("bmat", [P, SEQ], U0 + 4)
        cm = place("cmat", [P, SEQ], U0 + 6)
        sz = place("sz", [P, 2, SEQ], U0 + 8)
        xdt = place("xdt", [P, TT, BW], U0 + 12)
        qd = place("qd", [P, 2, SEQ], U0 + 16)
        kd = place("kd", [P, 2, SEQ], U0 + 20)
        vd = place("vd", [P, TT, BW], U0 + 24)
        adtb = place("adtb", [P, TT, P], U0 + 28, f32r)
        adtb_l = place("adtb_l", [P, TT, P], U0 + 30, f32r)
        upper_r = place("upper_r", [P, SEQ], Z0 + 4, f32r)
        ydh = place("ydh", [P, 2, SEQ], U0, f32r)
        ydl = place("ydl", [P, 2, SEQ], U0 + 4, f32r)
        qb = place("qb", [P, 2, SEQ], Z0 + 64)
        kb = place("kb", [P, 2, SEQ], Z0 + 68)
        vb = place("vb", [P, TT, BW], Z0 + 72)
        T0 = Z0 + 76
        gt = place("gt", [P, 2, SEQ], T0)
        xbuf = place("xbuf", [P, 4, SEQ + 3], T0)
        etmp = place("etmp", [P, SEQ], T0 + 8.25)
        sqjunk = place("sqjunk", [P, DM], T0)
        cbs = place("cbs", [P, 1280], T0 + 4)
        dec = place("dec", [P, 1280], T0 + 9)
        stl = place("stl", [P, 1280], T0 + 4)
        stsp = place("stsp", [P, 1280], T0 + 9)
        mp = place("mp", [P, 1280], T0 + 4)
        mpt = place("mpt", [P, 1280], T0 + 9)
        tri = place("tri", [P, 2 * P], T0 + 14.25, f32r)
        st_h = place("st_h", [P, 1280], U0 + 16, f32r)
        st_l = place("st_l", [P, 1280], U0 + 21, f32r)
        msq = place("msq", [P, 2, SEQ], Z0 + 28)
        mrs = place("mrs", [P, 2, SEQ], Z0 + 24)
        acc0 = place("acc0", [P, SEQ], Z0)
        sq0 = place("sq0", [P, 2, SEQ], Z0 + 2)
        ah = place("ah", [P, 8, SEQ], Z0, f32r)
        al = place("al", [P, 8, SEQ], Z0 + 16, f32r)
        fg_t = place("fg_t", [P, 2, SEQ], Z0 + 64)
        fu_t = place("fu_t", [P, 2, SEQ], Z0 + 68)
        acc1 = place("acc1", [P, SEQ], Z0 + 32)
        acc2 = place("acc2", [P, SEQ], Z0 + 34)
        sq1 = place("sq1", [P, 2, SEQ], Z0 + 36)
        sq2 = place("sq2", [P, 2, SEQ], Z0 + 40)
        r1 = place("r1", [P, SEQ], Z0 + 44)
        r2 = place("r2", [P, SEQ], Z0 + 46)
        cs2 = place("cs2", [P, 2, SEQ], 48)
        lng = place("lng", [P, DM], 52)
        lnb = place("lnb", [P, DM], 56)
        ath = place("ath", [P, KD, SEQ], Z0, f32r)
        atl = place("atl", [P, KD, SEQ], Z0 + 16, f32r)
        sgh = place("sgh", [P, KD, SEQ], Z0, f32r)
        sgl = place("sgl", [P, KD, SEQ], Z0 + 16, f32r)
        vg = place("vg", [P, TT, DM], Z0 + 32)
        rope_q = place("rope_q", [P, 2, SEQ], Z0 + 32)
        rope_t = place("rope_t", [P, 2, SEQ], Z0 + 36)
        za_e = place("za_e", [P, 2, SEQ], Z0 + 12)
        y2 = place("y2", [P, KD, SEQ], Z0 + 48)
        q2 = place("q2", [P, 4, SEQ], Z0 + 48)
        za = place("za", [P, 4, SEQ], Z0 + 56)
        za_last = place("za_last", [P, 2, SEQ], Z0 + 28)
        k2 = place("k2", [P, 2, SEQ], Z0 + 64)
        v2 = place("v2", [P, TT, GW], Z0 + 68)
        wp = place("wp", [P, 3, 2, 256], Z0 + 70)
        wpt = place("wpt", [P, 2, SEQ], Z0 + 76)
        att_t = place("att_t", [P, SEQ], Z0 + 80)
        g2t = place("g2t", [P, 2, SEQ], Z0 + 64)
        ub = place("ub", [P, 2, SEQ], Z0 + 64)
        zb = place("zb", [P, 2, SEQ], Z0 + 68)
        sgt = place("sgt", [P, 2, SEQ], Z0 + 72)
        y2h = place("y2h", [P, KD, SEQ], Z0 + 32, f32r)
        y2l = place("y2l", [P, KD, SEQ], Z0 + 64, f32r)
        D0 = Z0 + 82.25
        perm = place("perm", [P, P + 256], D0)
        bsb = place("bsb", [P, 8, P], D0 + 1.5)
        wT = place("wT", [P, 8, P], D0 + 5.5)
        sgw = place("sgw", [P, 8, P], Z0 + 70)
        g4t = place("g4t", [P, 2, SEQ], D0 + 1.5)
        acc3 = place("acc3", [P, SEQ], Z0)
        sq3 = place("sq3", [P, 2, SEQ], Z0 + 2)
        fo = place("fo", [P, 2, SEQ], Z0 + 8)
        ot = place("ot", [P, TT, DM], Z0 + 16)
        dtf = place("dtf", [HEADS, SEQ], Z0 + 28)
        wdt = place("wdt", [P, KD, HEADS], Z0 + 24)
        wdth = place("wdth", [P, KD, HEADS], Z0 + 25, f32r)
        wdtl = place("wdtl", [P, KD, HEADS], Z0 + 26, f32r)

        ident = c1[:, 0:128]
        upper = c1[:, 128:640]
        u_incl = c1[:, 128:256]
        ones = c1[:, 256:384]
        u_strict = c1[:, 640:768]
        t_after = c1[:, 768:896]
        negmask = c1[:, 896:1024]

        def pcol(name, i, n=1):
            return prm[:, PAR[name][0] + i:PAR[name][0] + i + n]

        ss = sml[:, 0:4]
        rcol = sml[:, 4:8]
        dtv = sml[:, 8:24]
        dta = sml[:, 24:40]
        dts = sml[:, 40:56]
        dts2 = sml[:, 56:72]
        dtq = sml[:, 72:88]
        adt = sml[:, 88:104]
        acs = sml[:, 104:120]
        ealog = sml[:, 120:124]
        fgng = sml[:, 124:132]
        mmx = sml[:, 132:136]
        mnm = sml[:, 136:140]
        mls = sml[:, 140:144]
        mrl = sml[:, 144:148]
        wmx = sml[:, 148:154]
        wnm = sml[:, 154:160]
        wls = sml[:, 160:166]
        wes = sml[:, 166:172]
        bns = sml[:, 172:220]
        mv = sml[:, 220:228]
        lrs = sml[:, 228:232]
        half_c = sml[:, 232:252]

        G = [ctx.enter_context(nc.psum_tensor(f"gemm{i}", [P, 512], f32)) for i in range(4)]
        M = [ctx.enter_context(nc.psum_tensor(f"mix{i}", [P, 512], f32)) for i in range(4)]

        STEPS, W_PER = KD * TT, 6

        def za_tile(m):
            return za[:, m % 4, :] if m < 6 else za_last[:, m - 6, :]

        def as_f32(ap):
            return ap.bitcast(f32)

        def cols(w, c0, n, k0=0, k=KD):
            return w[k0 * P:(k0 + k) * P, bass.ds(c0, n)].rearrange("(k p) c -> p k c", p=P)

        N_A = 12
        ORDER = (0, 2, 3, 1)
        N_B = 16
        n_b0, n_c0 = N_A, N_A + N_B
        n_d0 = n_c0 + 4
        ffn_units = []
        _n, _h = n_d0, 0
        for part in FFN_PARTS:
            ffn_units.append((_n, part, _h))
            _n += part + 4
            _h += part
        n_e0 = _n
        n_qz = n_e0 + 1
        n_vs = n_qz + 8
        n_ga = n_vs + 4
        n_uz = n_ga + 8
        n_gs = n_uz + 8
        n_o2 = n_gs + 8
        N_UNITS = n_o2 + 4

        def tiles_before(n):
            return 2 * n + 2 * min(max(n - n_b0, 0), N_B)

        def raw_count(n):
            def dmas(m):
                return 2 if n_b0 <= m < n_c0 or n_d0 <= m <= n_e0 else 1
            return 16 * sum(dmas(m) for m in range(n % 2, n + 1, 2))

        block = ctx.enter_context(nc.Block())

        @block.sync
        def _(sp):
            sp.dma_start(ident, cst1[:, 0:P]).then_inc(sem("start_in"), 16)
            sp.dma_start(prm[:, :], par).then_inc(sem("start_in"), 16)

            def load_x(q):
                sp.dma_start(xtm[:, :, q * 256:(q + 1) * 256],
                             x[:, q * 256:(q + 1) * 256].rearrange("(t p) c -> p t c", p=P)).then_inc(sem(f"x_in{q}"), 16)

            def load(n, src, dst=None):
                sp.dma_start(raw[:, n % 2] if dst is None else dst, src).then_inc(sem(f"raw_in{n % 2}"), 16)

            def slot_free(n):
                if n >= 2:
                    sp.wait_ge(sem("lo_done"), n - 1)

            a_cols = (IN_XA, IN_BG, IN_CG, IN_X, IN_BC, IN_Z, IN_QD, IN_KD, IN_VD, IN_QB, IN_KB, IN_VB)
            for n, c in enumerate(a_cols):
                slot_free(n)
                load(n, cols(w_in, c, UC))
                if n == 0:
                    for q in range(4):
                        load_x(q)
                    sp.dma_start(c1[:, P:], cst1[:, P:]).then_inc(sem("c1_in"), 16)
                if n == 1:
                    sp.dma_start(wdt[:, :, :], cols(w_in, IN_DT, HEADS)).then_inc(sem("wdt_in"), 16)

            def stream(n0, count, sources):
                with sp.Fori(0, count // 2) as i:
                    for j in range(2):
                        u, slot = 2 * i + j, (n0 + j) % 2
                        parts = sources(u, slot)
                        for src, _ in parts:
                            sp.lower_val(src.offset * 4)
                        sp.wait_ge(sem("lo_done"), u + (n0 - 1))
                        for src, dst in parts:
                            sp.dma_start(dst, src).then_inc(sem(f"raw_in{slot}"), 16)

            def tiles_of(w, c0, k0=0, k=KD, dst=raw, at=0):
                return lambda u, slot: (cols(w, u * UC + c0, UC, k0, k), dst[:, slot, at:at + k])

            def both(*of):
                return lambda u, slot: [f(u, slot) for f in of]

            for q, br in enumerate(ORDER):
                stream(n_b0 + 4 * q, 4, both(tiles_of(w_in, IN_G + br * DM), tiles_of(w_branch[br], 0, 0, 2, raw_b)))
            stream(n_c0, 4, both(tiles_of(w_o, 0)))
            sp.wait_ge(sem("tile_done"), tiles_before(n_c0))
            sp.dma_start(cs2[:, :, :], cst2a.rearrange("p (a s) -> p a s", a=2)).then_inc(sem("c2_in"), 16)
            sp.dma_start(lng[:, :], ln_g.partition_broadcast(P)).then_inc(sem("c2_in"), 16)
            sp.dma_start(lnb[:, :], ln_b.partition_broadcast(P)).then_inc(sem("c2_in"), 16)
            sp.wait_ge(sem("m_lo"), KD)
            sp.dma_start(perm[:, :], cst2b).then_inc(sem("c2_in"), 16)
            sp.dma_start(bsb[:, :, :].rearrange("p g i -> p (g i)"), sg_b.partition_broadcast(P)).then_inc(sem("c2_in"), 16)
            for n0, part, h0 in ffn_units:
                stream(n0, part, lambda u, slot: [(cols(w_gu, (u + h0) * P + c, P), raw[:, slot, :, at:at + P])
                                                  for c, at in ((0, 0), (FFN, P))])
                half = part // 2
                stream(n0 + part, 4, both(tiles_of(w_down, 0, h0, half), tiles_of(w_down, 0, h0 + half, part - half, raw, half)))
            slot_free(n_e0)
            for k in (0, 4):
                load(n_e0, cols(w_in2, I2_K, UC, k, 4), raw[:, n_e0 % 2, k:k + 4])
            sp.wait_ge(sem("tile_done"), tiles_before(n_e0))
            sp.dma_start(sgw[:, :, :], sg_w.rearrange("g i j -> i g j")).then_inc(sem("sgw_in"), 16)

            def stream_pairs(n0, first, second):
                with sp.Fori(0, 4) as p:
                    for j, (w, c0) in enumerate((first, second)):
                        slot = (n0 + j) % 2
                        src = cols(w, p * UC + c0, UC)
                        sp.lower_val(src.offset * 4)
                        sp.wait_ge(sem("lo_done"), 2 * p + (n0 + j - 1))
                        sp.dma_start(raw[:, slot], src).then_inc(sem(f"raw_in{slot}"), 16)

            stream_pairs(n_qz, (w_in2, I2_Q), (w_in2, I2_ZA))
            stream(n_vs, 4, both(tiles_of(w_in2, I2_VS)))
            stream_pairs(n_ga, (w_in2, I2_GA), (w_ao, 0))
            stream_pairs(n_uz, (w_in2, I2_U), (w_in2, I2_ZS))
            stream_pairs(n_gs, (w_in2, I2_GS), (w_so, 0))
            stream(n_o2, 4, both(tiles_of(w_o2, 0)))
            for t in range(TT):
                if t == 1:
                    sp.wait_ge(sem("out_act"), 1)
                else:
                    sp.wait_ge(sem("out_dve"), max(t, 1))
                sp.dma_start(out[t * P:(t + 1) * P, :], ot[:, t, :]).then_inc(sem("o_out"), 16)
            sp.wait_ge(sem("o_out"), 64)

        @block.gpsimd
        def _(pool):
            def rest(n, s, with_b=False):
                pool.wait_ge(sem("hi_done"), n + 1)
                a = lambda t: t[:, s].rearrange("p k c -> p (k c)")
                if with_b:
                    nc.gpsimd.tensor_tensor(a(wlo_b), a(raw_b), as_f32(a(whi_b)), ALU.subtract)
                nc.gpsimd.tensor_tensor(a(wlo), a(raw), as_f32(a(whi)), ALU.subtract).then_inc(sem("lo_done"), 1)

            def rests(n0, n1, with_b=False):
                if (n1 - n0) // 2:
                    with pool.Fori(0, (n1 - n0) // 2) as i:
                        for s in range(2):
                            rest(2 * i + n0 + s, (n0 + s) % 2, with_b)
                if (n1 - n0) % 2:
                    rest(n1 - 1, (n1 - 1) % 2, with_b)

            rests(0, n_b0)
            rests(n_b0, n_c0, True)
            rests(n_c0, N_UNITS)

        MIX = {11: [("dt",)], 12: [("dtT",)], 13: [("xsT",)], 14: [("acs",)], 15: [("cb", 0)], 16: [("mh1", 0)],
               17: [("mh2", 0), ("mh1", 1)], 18: [("mh2", 1)], 19: [("cb", 1), ("mh1", 2)],
               20: [("mh2", 2), ("mh1", 3)], 21: [("mh2", 3)], 22: [("mn", 0)], 23: [("mn", 1)]}
        for h in range(HEADS):
            for slots, st in (((25 + 2 * h, 26 + 2 * h, 27 + 2 * h), "mo"), ((34 + 3 * h, 36 + 3 * h, 37 + 3 * h), "st")):
                for i, at in enumerate(slots):
                    step = (f"{st}{i + 1}", h)
                    if i == 2:
                        MIX.setdefault(at, []).insert(0, step)
                    else:
                        MIX.setdefault(at, []).append(step)

        def run_mix(stages, slot):
            for name, *args in MIX.get(slot, []):
                stages[name](*args)

        @block.tensor
        def _(pe):
            mm = nc.tensor.matmul

            def gemm_fm(T, n, s, xh, xl, kts, col, first, whi_=whi, wlo_=wlo, hook=None, ready=None, turn=None):
                bank = G[T % 4] if isinstance(T, int) else G[T[1]]
                Tv = T if isinstance(T, int) else T[0]
                if not isinstance(T, int) or T >= 4:
                    pe.wait_ge(sem("tile_free"), Tv - 3)
                else:
                    pe.wait_ge(sem("xg_kept"), T + 1)
                if first:
                    pe.wait_ge(sem("hi_done"), n + 1)
                half = (3 * kts // 2 + 1) // 2
                for k in range(kts):
                    if turn and k in (2, 4):
                        turn(k + 2)
                        turn(k + 3)
                    if ready:
                        pe.wait_ge(sem(ready[0]), ready[1] + k + 1)
                    w = whi_[:, s, k, col:col + P]
                    mm(bank[:, :], w, xh[:, k, :], start=(k == 0), stop=False)
                    mm(bank[:, :], w, xl[:, k, :], start=False, stop=False)
                    if hook and k == half - 1:
                        hook()
                if first:
                    pe.wait_ge(sem("lo_done"), n + 1)
                for k in range(kts):
                    last = mm(bank[:, :], wlo_[:, s, k, col:col + P], xh[:, k, :], start=False, stop=(k == kts - 1))
                last.then_inc(sem("tile_done"), 1)

            def gemm_tm(T, n, c0, w_cols, per_bank, hook=None):
                bank, s = G[T % 4], n % 2
                pe.wait_ge(sem("tile_free"), T - 3)
                pe.wait_ge(sem("hi_done"), n + 1)
                pe.wait_ge(sem("lo_done"), n + 1)
                for i in range(per_bank):
                    t = i if per_bank == TT else (T % 2) * per_bank + i
                    o = bank[:, i * w_cols:(i + 1) * w_cols]
                    for k in range(KD):
                        w, tok = slice(c0, c0 + w_cols), slice(t * P, (t + 1) * P)
                        mm(o, hh[:, k, tok], whi[:, s, k, w], start=(k == 0), stop=False)
                        mm(o, hl[:, k, tok], whi[:, s, k, w], start=False, stop=False)
                        last = mm(o, hh[:, k, tok], wlo[:, s, k, w], start=False, stop=(k == KD - 1))
                    if i == per_bank - 1:
                        last.then_inc(sem("tile_done"), 1)
                    if hook:
                        hook()

            def unit_fm(n, xh=hh, xl=hl, kts=KD, after=None, hook=None, ready=None, turn=None):
                for j in range(2):
                    gemm_fm(tiles_before(n) + j, n, n % 2, xh, xl, kts, j * P, j == 0, hook=hook,
                            ready=None if j else ready, turn=None if j else turn)
                    if after:
                        after(j)

            pe.wait_ge(sem("start_in"), 32)

            def turn_in(m):
                pe.wait_ge(sem(f"x_in{m // 2}"), 16)
                for t in range(TT):
                    last = nc.tensor.transpose((G + M)[m][:, t * P:(t + 1) * P], xtm[:, t, m * P:(m + 1) * P], ident)
                last.then_inc(sem("xT_ps"), 1)

            for m in range(4):
                turn_in(m)

            def st_dt():
                pe.wait_ge(sem("wdt_lo"), 1)
                for k in range(KD):
                    o = M[0][0:HEADS, :]
                    mm(o, wdth[:, k, :], hh[:, k, :], start=(k == 0), stop=False)
                    mm(o, wdth[:, k, :], hl[:, k, :], start=False, stop=False)
                    last = mm(o, wdtl[:, k, :], hh[:, k, :], start=False, stop=(k == KD - 1))
                last.then_inc(sem("dt_ps"), 1)

            def st_dtT():
                pe.wait_ge(sem("dt_f"), 1)
                for t in range(TT):
                    last = nc.tensor.transpose(M[0][:, t * HEADS:(t + 1) * HEADS], dtf[0:HEADS, t * P:(t + 1) * P],
                                               ident[0:HEADS, 0:HEADS])
                last.then_inc(sem("dtT_ps"), 1)

            def st_xsT():
                pe.wait_ge(sem("silu"), 2)
                for b in range(2):
                    for i in range(2):
                        for f in range(2):
                            t = 2 * b + i
                            last = nc.tensor.transpose(M[1 + b][:, i * BW + f * P:i * BW + (f + 1) * P],
                                                       xs[:, f, t * P:(t + 1) * P], ident)
                    last.then_inc(sem("xsT_ps"), 1)

            def st_acs():
                pe.wait_ge(sem("adt"), 1)
                for n in range(TT):
                    o = M[3][:, n * HEADS:(n + 1) * HEADS]
                    for m in range(n + 1):
                        last = mm(o, u_incl if m == n else ones, adt[:, m * HEADS:(m + 1) * HEADS],
                                  start=(m == 0), stop=(m == n))
                last.then_inc(sem("acs_ps"), 1)

            def st_cb(g):
                pe.wait_ge(sem("silu"), 4)
                if g == 0:
                    pe.wait_ge(sem("dtv_read"), 1)
                    pe.wait_ge(sem("xdt"), 2)
                else:
                    pe.wait_ge(sem("y_mid"), 1)
                gs = slice(64 * g, 64 * g + 64)
                for n, (_, w) in enumerate(REG):
                    b, c = RBANK[n]
                    last = mm(M[b][:, c:c + w], bm[gs, n * P:(n + 1) * P], cm[gs, n * P:SEQ], start=True, stop=True)
                last.then_inc(sem("cb_ps"), 1)

            def st_mh1(h):
                pe.wait_ge(sem("adtb"), h + 1)
                if h == 0:
                    pe.wait_ge(sem("acs"), 1)
                    pe.wait_ge(sem("rounded_consts"), 3)
                else:
                    pe.wait_ge(sem("seg"), h)
                for m in range(TT):
                    for part in (adtb, adtb_l):
                        last = mm(M[3][:, m * P:SEQ], part[:, m, :], upper_r[:, 0:SEQ - m * P],
                                  start=(m == 0 and part is adtb), stop=(m == TT - 1 and part is adtb_l))
                last.then_inc(sem("acsb_ps"), 1)

            def st_mh2(h):
                pe.wait_ge(sem("mt"), h + 1)
                if h % 2 == 0:
                    pe.wait_ge(sem("cbs"), h // 2 + 1)
                o = M[0][64 * (h % 2):64 * (h % 2) + 64, :]
                for n, (a, w) in enumerate(REG):
                    last = mm(o[:, n * P:SEQ], xdt[:, n, h * DH:(h + 1) * DH], dec[:, a:a + w],
                              start=(n == 0), stop=(n == TT - 1))
                last.then_inc(sem("y_ps"), 1)

            def st_mn(g):
                pe.wait_ge(sem("y_sq"), g + 1)
                if g:
                    pe.wait_ge(sem("yrstd"), g)
                mm(M[1][:, :], ones, msq[:, g, :], start=True, stop=True).then_inc(sem("ysum_ps"), 1)

            def st_mo1(h):
                if h == 0:
                    pe.wait_ge(sem("tile_free"), tiles_before(9))
                    pe.wait_ge(sem("yc_lo"), 2)
                else:
                    pe.wait_ge(sem("mo_pt"), 3 * h)
                r, t = slice(64 * (h % 2), 64 * (h % 2) + 64), h // 2
                for c in (3, 2, 0, 1):
                    b, o = QBANK[c]
                    w = (c + 1) * P
                    last = mm(M[b][:, o:o + w], qd[r, t, c * P:(c + 1) * P], kd[r, t, 0:w], start=True, stop=True)
                last.then_inc(sem("mo_s"), 1)

            def st_mo2(h):
                pe.wait_ge(sem("mo_p"), h + 1)
                for n in (0, 1, 3, 2):
                    b, o = RBANK[n]
                    for c in range(n, TT):
                        a = QREG[c][0] + n * P
                        last = nc.tensor.transpose(M[b][:, o + (c - n) * P:o + (c - n + 1) * P], mp[:, a:a + P], ident)
                last.then_inc(sem("mo_t"), 1)

            def attend(o, v, probs, h, done):
                for n, (a, w) in enumerate(REG):
                    last = mm(o[:, n * P:SEQ], v[:, n, h * DH:(h + 1) * DH], probs[:, a:a + w],
                              start=(n == 0), stop=(n == TT - 1))
                last.then_inc(sem(done), 1)

            def st_mo3(h):
                pe.wait_ge(sem("mo_pt"), 3 * h + 3)
                if h == 2:
                    pe.wait_ge(sem("yd_lo"), 1)
                attend(M[3][64 * (h % 2):64 * (h % 2) + 64, :], vd, mpt, h, "mo_o")

            def st_st1(h):
                if h == 0:
                    pe.wait_ge(sem("tile_free"), tiles_before(12))
                    pe.wait_ge(sem("yd_lo"), 2)
                else:
                    pe.wait_ge(sem("st_arg"), h)
                r, t = slice(64 * (h % 2), 64 * (h % 2) + 64), h // 2
                for n in (0, 1, 3, 2):
                    b, o = RBANK[n]
                    last = mm(M[b][:, o:o + REG[n][1]], kb[r, t, n * P:(n + 1) * P], qb[r, t, n * P:SEQ], start=True, stop=True)
                last.then_inc(sem("st_z"), 1)

            def st_st2(h):
                pe.wait_ge(sem("rounded_consts"), 2)
                pe.wait_ge(sem("st_lo"), h + 1)
                for n in (0, 1, 3, 2):
                    b, o = RBANK[n]
                    a, w = REG[n]
                    for part in (st_h, st_l):
                        last = mm(M[b][:, o:o + w], tri[:, 0:P], part[:, a:a + w], start=(part is st_h),
                                  stop=(n == TT - 1 and part is st_l))
                    for m in range(n + 1, TT):
                        a, w = REG[m]
                        for part in (st_h, st_l):
                            last = mm(M[b][:, o + (m - n) * P:o + REG[n][1]], tri[:, P:], part[:, a:a + w],
                                      start=False, stop=(m == TT - 1 and part is st_l))
                last.then_inc(sem("st_b"), 1)

            def st_st3(h):
                pe.wait_ge(sem("st_w"), h + 1)
                if h == 2:
                    pe.wait_ge(sem("yb_lo"), 1)
                attend(M[3][64 * (h % 2):64 * (h % 2) + 64, :], vb, stl, h, "st_o")

            stages = {"dt": st_dt, "dtT": st_dtT, "xsT": st_xsT, "acs": st_acs, "cb": st_cb, "mh1": st_mh1, "mh2": st_mh2,
                      "mn": st_mn, "mo1": st_mo1, "mo2": st_mo2, "mo3": st_mo3, "st1": st_st1, "st2": st_st2,
                      "st3": st_st3}

            for n in range(N_A):
                def after(j, n=n):
                    if n == 0 and j == 1:
                        pe.wait_ge(sem("c1_in"), 16)
                        pe.wait_ge(sem("h_lo"), KD)
                        pe.wait_ge(sem("x_kept"), KD - 4)
                        pe.wait_ge(sem("rdiag"), 1)
                        for t in range(TT):
                            last = mm(M[0][:, t * P:(t + 1) * P], ones, xbuf[:, t, 0:P], start=True, stop=True)
                        last.then_inc(sem("r_ps"), 1)
                    run_mix(stages, 2 * n + j)
                if n in (8, 11):
                    for j in range(2):
                        gemm_tm(tiles_before(n) + j, n, 0, BW, 2)
                        after(j)
                else:
                    unit_fm(n, after=after, ready=("h_lo", 0) if n == 0 else None,
                            turn=turn_in if n == 0 else None)

            for i in range(N_B):
                n = n_b0 + i
                s = n % 2
                yhi, ylo = ((yh[0], yl[0]), (yh[1], yl[1]), (ydh, ydl), (yh[0], yl[0]))[i // 4]
                for j in range(2):
                    T = tiles_before(n) + 2 * j
                    gemm_fm(T, n, s, hh, hl, KD, j * P, j == 0)
                    if i % 4 == 0 and j == 0:
                        pe.wait_ge(sem(("ya_lo", "yc_lo", "yd_lo", "yb_lo")[i // 4]), 2)
                    gemm_fm(T + 1, n, s, yhi, ylo, 2, j * P, False, whi_b, wlo_b)
                    run_mix(stages, 24 + 2 * i + j)

            for p in range(4):
                unit_fm(n_c0 + p, mh, ml, ready=None if p else ("m_lo", 0))

            for f, (n0, part, h0) in enumerate(ffn_units):
                if f == 0:
                    gemm_fm(tiles_before(n0), n0, n0 % 2, hh, hl, KD, 0, True, ready=("h2_lo", 0))
                    pe.wait_ge(sem("acc0"), KD)
                    mm(M[0][:, :], ones, acc0[:, :], start=True, stop=True).then_inc(sem("n2_ps"), 1)
                    gemm_fm(tiles_before(n0) + 1, n0, n0 % 2, hh, hl, KD, P, False)
                    unit_fm(n0 + 1)
                with pe.Fori(1 if f == 0 else 0, part // 2) as i:
                    for s in range(2):
                        n = 2 * i + n0 + s
                        for j in range(2):
                            b = (tiles_before(n0) + 2 * s + j) % 4
                            gemm_fm((4 * i + tiles_before(n0) + 2 * s + j, b), n, (n0 + s) % 2, hh, hl, KD, j * P, j == 0)
                for p in range(4):
                    unit_fm(n0 + part + p, ah, al, part, ready=None if p else ("act_lo", h0))

            T = tiles_before(n_e0)
            gemm_fm(T, n_e0, n_e0 % 2, hh, hl, KD, 0, True, ready=("h3_lo", 0))
            pe.wait_ge(sem("acc2"), KD)
            mm(M[0][:, :], ones, acc1[:, :], start=True, stop=True)
            mm(M[1][:, :], ones, acc2[:, :], start=True, stop=True).then_inc(sem("n3_ps"), 1)
            gemm_fm(T + 1, n_e0, n_e0 % 2, hh, hl, KD, P, False)

            def turn_rows():
                pe.wait_ge(sem("R3"), 1)
                for t in range(TT):
                    last = nc.tensor.transpose(M[2][:, t * P:(t + 1) * P], R[:, t * P:(t + 1) * P], ident)
                last.then_inc(sem("rcol_ps"), 1)
                pe.wait_ge(sem("sgw_in"), 16)
                for g in range(8):
                    last = nc.tensor.transpose(M[g // 4][:, (g % 4) * P:(g % 4 + 1) * P], sgw[:, g, :], ident)
                last.then_inc(sem("wT_ps"), 1)

            def turn_keys():
                pe.wait_ge(sem("tile_free"), tiles_before(n_e0) + 1)
                mm(M[3][:, :], perm[:, 0:P], rope_q[:, 0, :], start=True, stop=True).then_inc(sem("rope_ps"), 1)
                pe.wait_ge(sem("rcol_read"), 1)
                pe.wait_ge(sem("tile_free"), tiles_before(n_e0) + 2)
                for t in range(TT):
                    last = nc.tensor.transpose(M[2][:, t * P:(t + 1) * P], rope_t[:, 1, t * P:(t + 1) * P], ident)
                last.then_inc(sem("v2_ps"), 1)

            pos = [0]

            def keys_of(c):
                return (1,) if c == 0 else (0, 1)

            def w_scores(s):
                m, c = s // TT, s % TT
                if s % 8 == 0:
                    pe.wait_ge(sem("tile_free"), tiles_before(n_qz + s // 4) + 2)
                if s == 0:
                    pe.wait_ge(sem("k_ready"), 1)
                if s >= 1:
                    pe.wait_ge(sem("w_s"), s)
                kv = m // 4
                for h in range(2):
                    r = slice(64 * h, 64 * h + 64)
                    k0 = max(c - 1, 0) * P
                    o = P if c == 0 else 0
                    last = mm(M[h][:, o:256], q2[r, m % 4, c * P:(c + 1) * P], k2[r, kv, k0:(c + 1) * P],
                              start=True, stop=True)
                last.then_inc(sem("w_ps"), 1)

            def w_turn(s):
                m, c = s // TT, s % TT
                pe.wait_ge(sem("w_p"), s + 1)
                if s >= 1:
                    pe.wait_ge(sem("w_pt"), s)
                for h in range(2):
                    for kb_ in keys_of(c):
                        last = nc.tensor.transpose(M[2][:, (2 * h + kb_) * P:(2 * h + kb_ + 1) * P],
                                                   wp[:, s % 3, h, kb_ * P:(kb_ + 1) * P], ident)
                last.then_inc(sem("w_t"), 1)

            def w_values(s):
                m, c = s // TT, s % TT
                pe.wait_ge(sem("w_pt"), s + 1)
                if c == 0 and m >= 1:
                    pe.wait_ge(sem("w_o"), m)
                kv = m // 4
                for h in range(2):
                    for kb_ in keys_of(c):
                        last = mm(M[3][64 * h:64 * h + 64, c * P:(c + 1) * P], v2[:, c - 1 + kb_, kv * DH:(kv + 1) * DH],
                                  wpt[:, s % 2, (2 * h + kb_) * P:(2 * h + kb_ + 1) * P],
                                  start=(kb_ == keys_of(c)[0]), stop=(kb_ == 1))
                last.then_inc(sem("w_v"), 1)

            def w_slot(limit):
                i = pos[0]
                if i >= limit and limit < STEPS:
                    return
                if 0 <= i - 4 < STEPS:
                    w_values(i - 4)
                if 0 <= i - 3 < STEPS:
                    w_turn(i - 3)
                if i < STEPS:
                    w_scores(i)
                pos[0] += 1

            for p in range(4):
                n = n_qz + 2 * p
                lim = W_PER * p
                for u in range(2):
                    for j in range(2):
                        gemm_fm(tiles_before(n + u) + j, n + u, (n + u) % 2, hh, hl, KD, j * P, j == 0,
                                hook=lambda: w_slot(lim))
                        if p == 0 and u == 0:
                            (turn_rows, turn_keys)[j]()
                        if u == 1 and j == 0:
                            for i in range(2):
                                pe.wait_ge(sem("rope_in"), 2 * p + i + 1)
                                mm(G[(tiles_before(n) + i) % 4][:, :], perm[:, 0:P], rope_q[:, i, :],
                                   start=True, stop=True).then_inc(sem("rope_ps"), 1)
                        if j == 0:
                            w_slot(lim)
            for p in range(4):
                n = n_vs + p
                for j in range(2):
                    gemm_tm(tiles_before(n) + j, n, 0, UC, 2, hook=lambda: w_slot(STEPS))

            def pairs_after_first(n0, xh, xl):
                with pe.Fori(1, 4) as p:
                    for u, (h, l) in enumerate(((hh, hl), (xh, xl))):
                        for j in range(2):
                            T = tiles_before(n0 + u) + j
                            gemm_fm((4 * p + T, T % 4), 2 * p + n0 + u, (n0 + u) % 2, h, l, KD, j * P, j == 0)

            unit_fm(n_ga, hook=lambda: w_slot(STEPS), after=lambda j: w_slot(STEPS))
            unit_fm(n_ga + 1, ath, atl, ready=("at_lo", 0))
            pairs_after_first(n_ga, ath, atl)

            for p in range(4):
                unit_fm(n_uz + 2 * p)
                if p == 0:
                    pe.wait_ge(sem("vb_ready"), TT)
                    pe.wait_ge(sem("wT_ready"), 1)
                for j in range(2):
                    m = 2 * p + j
                    if m >= 2:
                        pe.wait_ge(sem("mixed"), m - 1)
                    for t in range(TT):
                        last = mm(M[m % 2][:, t * P:(t + 1) * P], vg[:, t, m * P:(m + 1) * P], wT[:, m, :],
                                  start=True, stop=True)
                    last.then_inc(sem("mixed_ps"), 1)
                unit_fm(n_uz + 2 * p + 1)

            unit_fm(n_gs)
            unit_fm(n_gs + 1, sgh, sgl, ready=("sg_lo", 0))
            pairs_after_first(n_gs, sgh, sgl)

            def turn_out(m):
                pe.wait_ge(sem("fo"), m + 1)
                if m >= 3:
                    pe.wait_ge(sem("o_copied"), m - 2)
                for t in range(TT):
                    last = nc.tensor.transpose(M[1 + m % 3][:, t * P:(t + 1) * P], fo[:, m % 2, t * P:(t + 1) * P], ident)
                last.then_inc(sem("o_ps"), 1)

            for p in range(4):
                unit_fm(n_o2 + p, y2h, y2l, ready=None if p else ("y2_lo", 0),
                        after=lambda j: turn_out(2 * p + j - 1) if 2 * p + j else None)
            turn_out(KD - 1)
            pe.wait_ge(sem("acc3"), KD)
            for t in range(TT):
                last = mm(M[0][:, t:t + 1], acc3[:, t * P:(t + 1) * P], ones[:, 0:1], start=True, stop=True)
            last.then_inc(sem("n4_ps"), 1)

        @block.scalar
        def _(act):
            fn = nc.scalar.activation

            def split(n, i=0):
                if n >= N_UNITS:
                    return
                act.wait_ge(sem(f"raw_in{n % 2}"), 32 * i + raw_count(n))
                if n >= 2:
                    act.wait_ge(sem("tile_done"), 4 * i + tiles_before(n - 1))
                s = n % 2
                a = lambda t: t[:, s].rearrange("p k c -> p (k c)")
                if n_b0 <= n < n_c0:
                    fn(a(whi_b), a(raw_b), ACT.Copy)
                fn(a(whi), a(raw), ACT.Copy).then_inc(sem("hi_done"), 1)

            links = [0]

            def link(ins):
                links[0] += 1
                ins.then_inc(sem("act_link"), 1)
                act.wait_ge(sem("act_link"), links[0])

            def rsqrt(dst, mean_of, n):
                link(fn(dst, mean_of, ACT.Ln, scale=1.0 / n, bias=pcol("eps", 0)))
                return fn(dst, dst, ACT.Exp, scale=-0.5)

            def tanh(dst, src, scale=1.0):
                return fn(dst, src, ACT.Tanh, scale=scale)

            act.preload_act_table_set(EXP_LN)
            split(0)
            act.wait_ge(sem("start_in"), 32)
            for m in range(KD):
                act.wait_ge(sem("xT_ps"), m + 1)
                fn(hh[:, m, :], (G + M)[m][:, :], ACT.Copy, scale=pcol("g1", m)).then_inc(sem("h_hi"), 1)
            for m in range(4, KD):
                act.wait_ge(sem("h_lo"), m + 1)
                fn(xT[:, m, :], M[m - 4][:, :], ACT.Copy).then_inc(sem("x_kept"), 1)
            split(1)
            for t in range(TT):
                if t >= 1:
                    act.wait_ge(sem("ss"), t)
                fn(sqjunk[:, :], xtm[:, t, :], ACT.Square, accum_out=ss[:, t:t + 1]).then_inc(sem("ss"), 1)
            act.wait_ge(sem("ss"), TT)
            rsqrt(rcol, ss, DM).then_inc(sem("rcol"), 1)
            act.wait_ge(sem("wdt_in"), 16)
            flat = lambda t: t[:, :, :].rearrange("p k c -> p (k c)")
            fn(flat(wdth), flat(wdt), ACT.Copy).then_inc(sem("wdt_hi"), 1)
            fn(ealog, pcol("alog", 0, 4), ACT.Exp).then_inc(sem("ealog"), 1)
            act.preload_act_table_set(EXP_TANH)
            act.wait_ge(sem("c1_in"), 16)
            fn(tri[:, 0:P], t_after, ACT.Copy).then_inc(sem("rounded_consts"), 1)
            fn(tri[:, P:], ones, ACT.Copy).then_inc(sem("rounded_consts"), 1)

            def st_dtT():
                act.wait_ge(sem("dt_abs"), 1)
                fn(dta, dta, ACT.Exp, scale=-1.0).then_inc(sem("dt_exp"), 1)

            def st_cb(g):
                act.wait_ge(sem("cb_ps"), g + 1)
                if g == 1:
                    act.wait_ge(sem("mt"), 2)
                for b, c, a, w in RUNS:
                    last = fn(cbs[:, a:a + w], M[b][:, c:c + w], ACT.Copy)
                last.then_inc(sem("cb_sb"), 1)

            def st_mh1(h):
                act.wait_ge(sem("seg"), h + 1)
                fn(dec[:, :], dec[:, :], ACT.Exp).then_inc(sem("decay"), 1)

            def st_mn(g):
                act.wait_ge(sem("ysum_ps"), g + 1)
                act.preload_act_table_set(EXP_LN)
                rsqrt(mrs[:, g, :], M[1][:, :], P).then_inc(sem("yrstd"), 1)
                act.preload_act_table_set(EXP_TANH)
                act.wait_ge(sem("yn"), g + 1)
                fn(yh[1][:, g, :], sz[:, g, :], ACT.Copy).then_inc(sem("yc_hi"), 1)

            def st_mo1(h):
                act.wait_ge(sem("mo_nm"), h + 1)
                if h >= 1:
                    act.wait_ge(sem("mo_t"), h)
                for c in range(TT):
                    b, o = QBANK[c]
                    a, w = QREG[c]
                    last = fn(mp[:, a:a + w], M[b][:, o:o + w], ACT.Exp, bias=mnm[:, c:c + 1], accum_out=mls[:, c:c + 1])
                last.then_inc(sem("mo_e"), 1)

            def st_mo2(h):
                act.wait_ge(sem("mo_t"), h + 1)
                if h >= 1:
                    act.wait_ge(sem("mo_o"), h)
                for b, c, a, w in (RUNS[0], RUNS[2]):
                    fn(mpt[:, a:a + w], M[b][:, c:c + w], ACT.Copy).then_inc(sem("mo_pt"), 1)
                for b, c, a, w in (RUNS[1], RUNS[3]):
                    last = fn(mpt[:, a:a + w], M[b][:, c:c + w], ACT.Copy)
                last.then_inc(sem("mo_pt"), 1)

            def out_hi(bank, done, dst, name, h):
                if h % 2:
                    act.wait_ge(sem(done), h + 1)
                    fn(dst[:, h // 2, :], bank[:, :], ACT.Copy).then_inc(sem(name), 1)

            def st_mo3(h):
                out_hi(M[3], "mo_o", ydh, "yd_hi", h)

            def st_st1(h):
                act.preload_act_table_set(EXP_LN)
                act.wait_ge(sem("st_z"), h + 1)
                if h >= 1:
                    act.wait_ge(sem("st_o"), h)
                for i, (b, c, a, w) in enumerate(RUNS):
                    last = fn(stl[:, a:a + w], M[b][:, c:c + w], ACT.Abs)
                last.then_inc(sem("st_abs"), 1)
                act.wait_ge(sem("st_abs"), h + 1)
                fn(stl[:, :], stl[:, :], ACT.Exp, scale=-1.0).then_inc(sem("st_exp"), 1)
                act.wait_ge(sem("st_exp"), h + 1)
                fn(stl[:, :], stl[:, :], ACT.Ln, bias=1.0).then_inc(sem("st_ln"), 1)
                act.preload_act_table_set(EXP_TANH)

                act.wait_ge(sem("st_sp"), h + 1)
                if h >= 1:
                    act.wait_ge(sem("st_b"), h)
                fn(st_h[:, :], stsp[:, :], ACT.Copy).then_inc(sem("st_hi"), 1)

            def st_st2(h):
                act.wait_ge(sem("st_arg"), h + 1)
                fn(stl[:, :], stl[:, :], ACT.Exp).then_inc(sem("st_we"), 1)

            def st_st3(h):
                out_hi(M[3], "st_o", yh[0], "yb_hi", h)

            none = lambda *a: None
            stages = {"dt": none, "dtT": st_dtT, "xsT": none, "acs": none, "cb": st_cb, "mh1": st_mh1, "mh2": none, "mn": st_mn,
                      "mo1": st_mo1, "mo2": st_mo2, "mo3": st_mo3, "st1": st_st1, "st2": st_st2, "st3": st_st3}

            def st_mh2(h):
                if h % 2:
                    act.wait_ge(sem("y_mid"), h // 2 + 1)
                    fn(msq[:, h // 2, :], sz[:, h // 2, :], ACT.Square).then_inc(sem("y_sq"), 1)
            stages["mh2"] = st_mh2

            for n in range(N_A):
                for j in range(2):
                    if j == 0 and n >= 1:
                        split(n + 1)
                    i = 2 * n + j - 7
                    if 0 <= i < 6:
                        if i >= 1:
                            act.wait_ge(sem("silu"), i)
                        if i >= 4:
                            act.wait_ge(sem("tile_free"), tiles_before(5) + i - 3)
                            src = sz[:, i - 4, :]
                        else:
                            act.wait_ge(sem("silu_in"), i + 1)
                            src = (xs[:, 0, :], xs[:, 1, :], bm[:, :], cm[:, :])[i]
                        tanh(etmp[:, :], src).then_inc(sem("silu_tanh"), 1)
                    if n == 2 and j == 1:
                        for f in range(2):
                            act.wait_ge(sem("ya"), f + 1)
                            fn(yh[0][:, f, :], xa[:, f, :], ACT.Copy).then_inc(sem("ya_hi"), 1)
                        fn(upper_r[:, :], upper, ACT.Copy).then_inc(sem("rounded_consts"), 1)
                    run_mix(stages, 2 * n + j)

            for i in range(N_B):
                n = n_b0 + i
                for j in range(2):
                    t = 2 * i + j
                    if j == 0:
                        split(n + 1)
                    act.wait_ge(sem("tile_free"), tiles_before(n) + 2 * j + 1)
                    tanh(gt[:, t % 2, :], gt[:, t % 2, :], 0.5).then_inc(sem("gate"), 1)
                    if i // 4 == 3:
                        m = t - 24
                        act.wait_ge(sem("m_sum"), m + 1)
                        fn(mh[:, m, :], merged[:, m, :], ACT.Copy, scale=0.5).then_inc(sem("m_hi"), 1)
                    run_mix(stages, 24 + t)

            for p in range(4):
                for j in range(2):
                    m = 2 * p + j
                    if j == 0:
                        split(n_c0 + p + 1)
                    act.wait_ge(sem("tile_free"), tiles_before(n_c0) + m + 1)
                    if m >= 2:
                        act.wait_ge(sem("acc0"), m - 1)
                    fn(sq0[:, m % 2, :], xT[:, m, :], ACT.Square).then_inc(sem("sq0"), 1)
                    fn(hh[:, m, :], xT[:, m, :], ACT.Copy, scale=pcol("g2", m)).then_inc(sem("h2_hi"), 1)
            act.preload_act_table_set(EXP_LN)
            act.wait_ge(sem("n2_ps"), 1)
            rsqrt(R[:, :], M[0][:, :], DM).then_inc(sem("R2"), 1)

            for f, (n0, part, h0) in enumerate(ffn_units):
                with act.Fori(0, part // 2) as i:
                    for j in range(2):
                        n = n0 + j
                        split(n + 1, i)
                        act.wait_ge(sem("tile_free"), 4 * i + tiles_before(n) + 1)
                        fn(fg_t[:, n % 2, :], fg_t[:, n % 2, :], ACT.Silu).then_inc(sem("gate_act"), 1)
                if f < len(FFN_PARTS) - 1:
                    with act.Fori(0, 2) as i:
                        for j in range(2):
                            split(n0 + part + j + 1, i)
                    continue
                for m in range(KD):
                    n = n0 + part + m // 2
                    if m % 2 == 0:
                        split(n + 1)
                    act.wait_ge(sem("tile_free"), tiles_before(n) + m % 2 + 1)
                    if m >= 2:
                        act.wait_ge(sem("acc2"), m - 1)
                    fn(sq1[:, m % 2, :], xT[:, m, :], ACT.Square)
                    fn(sq2[:, m % 2, :], xT[:, m, :], ACT.Square, scale=pcol("fg", m)).then_inc(sem("sq12"), 1)
                    fn(hh[:, m, :], xT[:, m, :], ACT.Copy, scale=fgng[:, m:m + 1]).then_inc(sem("h3_hi"), 1)
            split(n_e0 + 1)
            act.preload_act_table_set(EXP_LN)
            act.wait_ge(sem("n3_ps"), 1)
            link(fn(r1[:, :], M[0][:, :], ACT.Ln, scale=1.0 / DM, bias=pcol("eps", 0)))
            fn(r2[:, :], r1[:, :], ACT.Exp, scale=-1.0).then_inc(sem("r1_sq"), 1)
            act.wait_ge(sem("r1_sq"), 1)
            fn(r1[:, :], r1[:, :], ACT.Exp, scale=-0.5).then_inc(sem("r1"), 1)
            act.wait_ge(sem("n3_var"), 1)
            rsqrt(r2[:, :], r2[:, :], DM).then_inc(sem("r2"), 1)
            act.preload_act_table_set(EXP_TANH)

            pos = [0]

            def w_exp(s):
                act.wait_ge(sem("w_nm"), s + 1)
                b = 2 * (s % 3)
                c0 = P if s % TT == 0 else 0
                for h in range(2):
                    fn(wp[:, s % 3, h, c0:256], wp[:, s % 3, h, c0:256], ACT.Exp, bias=wnm[:, b + h:b + h + 1],
                       accum_out=wls[:, b + h:b + h + 1])
                fn(wes[:, b:b + 2], wes[:, b:b + 2], ACT.Exp).then_inc(sem("w_e"), 1)

            def w_turned(s):
                act.wait_ge(sem("w_t"), s + 1)
                if s >= 2:
                    act.wait_ge(sem("w_v"), s - 1)
                if s % TT == 0:
                    for h in range(2):
                        last = fn(wpt[:, s % 2, (2 * h + 1) * P:(2 * h + 2) * P], M[2][:, (2 * h + 1) * P:(2 * h + 2) * P], ACT.Copy)
                else:
                    last = fn(wpt[:, s % 2, :], M[2][:, :], ACT.Copy)
                last.then_inc(sem("w_pt"), 1)

            def w_out(s):
                if s % TT == TT - 1:
                    m = s // TT
                    act.wait_ge(sem("w_o"), m + 1)
                    fn(ath[:, m, :], att_t[:, :], ACT.Copy).then_inc(sem("at_hi"), 1)

            def w_slot(limit):
                i = pos[0]
                if i >= limit and limit < STEPS:
                    return
                if 0 <= i - 4 < STEPS:
                    w_out(i - 4)
                if 0 <= i - 3 < STEPS:
                    w_turned(i - 3)
                if i < STEPS:
                    w_exp(i)
                pos[0] += 1

            def attention_gate(m):
                act.wait_ge(sem("tile_free"), tiles_before(n_qz + m // 2 * 2 + 1) + m % 2 + 1)
                if m >= 2:
                    act.wait_ge(sem("za"), m - 1)
                tanh(za_e[:, m % 2, :], za_tile(m)).then_inc(sem("za_e"), 1)

            for p in range(4):
                n = n_qz + 2 * p
                lim = W_PER * p
                for u in range(2):
                    for j in range(2):
                        w_slot(lim)
                        if j == 0:
                            split(n + u + 1)
                            w_slot(lim)
                        if u == 1 and j == 1:
                            attention_gate(2 * p)
                        if u == 0 and j == 0 and p >= 1:
                            attention_gate(2 * p - 1)
            for p in range(4):
                split(n_vs + p + 1)
                for i in range(4):
                    w_slot(STEPS)
                    if i == 1 and p == 0:
                        attention_gate(KD - 1)
            split(n_ga + 1)
            while pos[0] < STEPS + 5:
                w_slot(STEPS)

            for t in range(TT):
                act.wait_ge(sem("tile_free"), tiles_before(n_vs + 4))
                fn(vg[:, t, :], vg[:, t, :], ACT.Gelu).then_inc(sem("vs_act"), 1)
            act.wait_ge(sem("ln_var"), 1)
            fn(lrs, lrs, ACT.Sqrt).then_inc(sem("ln_rs"), 1)

            def gates(n0, buf, i0, bias0):
                for p in range(4):
                    for u in range(2):
                        if n0 != n_ga or p + u > 0:
                            split(n0 + 2 * p + u + 1)
                        if u == 0:
                            for j in range(2):
                                m = 2 * p + j
                                act.wait_ge(sem("tile_free"), tiles_before(n0 + 2 * p) + j + 1)
                                fn(buf[:, j, :], buf[:, j, :], ACT.Sigmoid, bias=pcol("bm", bias0 + m)).then_inc(sem("gm_act"), 1)
                        elif i0:
                            for j in range(2):
                                m = 2 * p + j
                                act.wait_ge(sem("y2_sum"), m + 1)
                                fn(y2h[:, m, :], y2[:, m, :], ACT.Copy).then_inc(sem("y2_hi"), 1)

            gates(n_ga, g2t, 0, 0)
            for p in range(4):
                n = n_uz + 2 * p
                split(n + 1)
                for j in range(2):
                    act.wait_ge(sem("tile_free"), tiles_before(n) + j + 1)
                    fn(ub[:, j, :], ub[:, j, :], ACT.Gelu).then_inc(sem("u_act"), 1)
                split(n + 2)
                for j in range(2):
                    act.wait_ge(sem("tile_free"), tiles_before(n + 1) + j + 1)
                    fn(zb[:, j, :], zb[:, j, :], ACT.Silu).then_inc(sem("zs_act"), 1)
                for j in range(2):
                    m = 2 * p + j
                    act.wait_ge(sem("sg"), m + 1)
                    fn(sgh[:, m, :], sgt[:, j, :], ACT.Copy).then_inc(sem("sg_hi"), 1)
            gates(n_gs, g4t, 1, 8)
            act.preload_act_table_set(EXP_LN)

            def copy_out(m):
                act.wait_ge(sem("o_ps"), m + 1)
                fn(ot[:, :, m * P:(m + 1) * P], M[1 + m % 3][:, :].rearrange("p (t c) -> p t c", t=TT), ACT.Copy)\
                    .then_inc(sem("o_copied"), 1)

            for p in range(4):
                split(n_o2 + p + 1)
                for j in range(2):
                    m = 2 * p + j
                    act.wait_ge(sem("tile_free"), tiles_before(n_o2) + m + 1)
                    if m >= 2:
                        act.wait_ge(sem("acc3"), m - 1)
                    fn(sq3[:, m % 2, :], xT[:, m, :], ACT.Square).then_inc(sem("sq3"), 1)
                    if m >= 1:
                        copy_out(m - 1)
            copy_out(KD - 1)
            act.wait_ge(sem("n4_ps"), 1)
            rsqrt(rcol, M[0][:, 0:TT], DM).then_inc(sem("R4"), 1)
            act.wait_ge(sem("R4"), 1)
            act.wait_ge(sem("o_copied"), KD)
            fn(ot[:, 1, :], ot[:, 1, :], ACT.Copy, scale=rcol[:, 1:2]).then_inc(sem("out_act"), 1)

        @block.vector
        def _(dve):
            v = nc.vector
            tt, ts, stt = v.tensor_tensor, v.tensor_scalar, v.scalar_tensor_tensor
            links = [0]

            def link(ins):
                links[0] += 1
                ins.then_inc(sem("dve_link"), 1)
                dve.wait_ge(sem("dve_link"), links[0])

            def tile_ready(T):
                dve.wait_ge(sem("tile_done"), T + 1)

            def scaled(T, dst, scale=None):
                tile_ready(T)
                if scale is None:
                    ins = tt(dst, G[T % 4][:, :], R[:, :], ALU.mult)
                else:
                    ins = stt(out=dst, in0=G[T % 4][:, :], scalar=scale, in1=R[:, :], op0=ALU.mult, op1=ALU.mult)
                ins.then_inc(sem("tile_free"), 1)
                dve.wait_ge(sem("tile_free"), T + 1)

            def scaled_tm(T, dsts, w):
                tile_ready(T)
                for i, (t, dst) in enumerate(dsts):
                    last = ts(dst, G[T % 4][:, i * w:(i + 1) * w], rcol[:, t:t + 1], None, ALU.mult)
                last.then_inc(sem("tile_free"), 1)

            dve.wait_ge(sem("start_in"), 32)
            for m in range(KD):
                dve.wait_ge(sem("h_hi"), m + 1)
                stt(out=hl[:, m, :], in0=(G + M)[m][:, :], scalar=pcol("g1", m), in1=as_f32(hh[:, m, :]),
                    op0=ALU.mult, op1=ALU.subtract).then_inc(sem("h_lo"), 1)
                for g in {0: (0,), KD - 1: (1, 2, 3)}.get(m, ()):
                    v.tensor_copy(xT[:, g, :], G[g][:, :]).then_inc(sem("xg_kept"), 1)
            ts(half_c, pcol("cw", 0, 20), 0.5, None, ALU.mult)
            tt(fgng, pcol("fg", 0, 8), pcol("ng2", 0, 8), ALU.mult)
            dve.wait_ge(sem("rcol"), 1)
            for t in range(TT):
                last = ts(xbuf[:, t, 0:P], ident, rcol[:, t:t + 1], None, ALU.mult)
            last.then_inc(sem("rdiag"), 1)
            dve.wait_ge(sem("r_ps"), 1)
            link(v.tensor_copy(R[:, :], M[0][:, :]))
            v.memset(cbuf[:, :, 0:2], 0.0)
            link(v.memset(xbuf[:, :, 0:3], 0.0))
            dve.wait_ge(sem("wdt_hi"), 1)
            flat = lambda t: t[:, :, :].rearrange("p k c -> p (k c)")
            tt(flat(wdtl), flat(wdt), as_f32(flat(wdth)), ALU.subtract).then_inc(sem("wdt_lo"), 1)

            def conv_a(f):
                link(tt(cbuf[:, f, 2:], cbuf[:, f, 2:], xa[:, f, :], ALU.mult))
                link(ts(xa[:, f, :], cbuf[:, f, 0:SEQ], pcol("ca", f), None, ALU.mult))
                for k in (1, 2):
                    link(stt(out=xa[:, f, :], in0=cbuf[:, f, k:k + SEQ], scalar=pcol("ca", 2 * k + f), in1=xa[:, f, :],
                             op0=ALU.mult, op1=ALU.add))
                tt(xa[:, f, :], xa[:, f, :], bgate[:, f, :], ALU.mult).then_inc(sem("ya"), 1)

            def silu_out(i, dst, val):
                dve.wait_ge(sem("silu_tanh"), i + 1)
                stt(out=dst, in0=etmp[:, :], scalar=1.0, in1=val, op0=ALU.add, op1=ALU.mult).then_inc(sem("silu"), 1)

            conv_dst = [xs[:, 0, :], xs[:, 1, :], bm[:, :], cm[:, :]]

            def conv_c(f):
                d = conv_dst[f]
                link(ts(d, xbuf[:, f, 0:SEQ], half_c[:, f:f + 1], half_c[:, 16 + f:17 + f], ALU.mult, ALU.add))
                for k in (1, 2, 3):
                    last = stt(out=d, in0=xbuf[:, f, k:k + SEQ], scalar=half_c[:, 4 * k + f:4 * k + f + 1], in1=d, op0=ALU.mult, op1=ALU.add)
                    if k < 3:
                        link(last)
                last.then_inc(sem("silu_in"), 1)

            def st_dt():
                dve.wait_ge(sem("dt_ps"), 1)
                tt(dtf[:, :], M[0][0:HEADS, :], R[0:HEADS, :], ALU.mult).then_inc(sem("dt_f"), 1)

            def st_dtT():
                dve.wait_ge(sem("dtT_ps"), 1)
                for t in range(TT):
                    a = slice(t * HEADS, (t + 1) * HEADS)
                    last = tt(dtv[:, a], M[0][:, a], pcol("dtb", 0, 4), ALU.add)
                last.then_inc(sem("dtv_read"), 1)
                dve.wait_ge(sem("dtv_read"), 1)
                link(ts(dts, dtv, -1.0, None, ALU.mult))
                tt(dta, dtv, dts, ALU.max).then_inc(sem("dt_abs"), 1)
                dve.wait_ge(sem("dt_exp"), 1)
                link(ts(dts, dta, 2.0, None, ALU.add))
                link(v.reciprocal(dts, dts))
                link(tt(dts, dta, dts, ALU.mult))
                link(tt(dts2, dts, dts, ALU.mult))
                link(ts(dtq, dts2, 1.0 / 17, None, ALU.mult))
                for d in (15, 13, 11, 9, 7, 5, 3):
                    link(stt(out=dtq, in0=dtq, scalar=1.0 / d, in1=dts2, op0=ALU.add, op1=ALU.mult))
                link(stt(out=dtq, in0=dtq, scalar=1.0, in1=dts, op0=ALU.add, op1=ALU.mult))
                link(ts(dtv, dtv, 0.0, None, ALU.max))
                link(stt(out=dtv, in0=dtq, scalar=2.0, in1=dtv, op0=ALU.mult, op1=ALU.add))
                dve.wait_ge(sem("ealog"), 1)
                stt(out=adt.rearrange("p (t h) -> p t h", h=HEADS), in0=dtv.rearrange("p (t h) -> p t h", h=HEADS), scalar=-1.0,
                    in1=ealog.unsqueeze(1).broadcast_to((P, TT, HEADS)), op0=ALU.mult, op1=ALU.mult).then_inc(sem("adt"), 1)

            def spread(h):
                dve.wait_ge(sem("adt"), 1)
                if h >= 1:
                    dve.wait_ge(sem("acsb_ps"), h)
                a = adt.rearrange("p (t h) -> p t h", h=HEADS)[:, :, h:h + 1]
                wide = a.broadcast_to((P, TT, P))
                link(v.tensor_copy(adtb[:, :, :], wide))
                tt(adtb_l[:, :, :], wide, as_f32(adtb[:, :, :]), ALU.subtract).then_inc(sem("adtb"), 1)

            def st_xsT():
                for b in range(2):
                    dve.wait_ge(sem("xsT_ps"), b + 1)
                    for i in range(2):
                        t = 2 * b + i
                        d = dtv[:, t * HEADS:(t + 1) * HEADS].unsqueeze(2).broadcast_to((P, HEADS, DH))
                        last = tt(xdt[:, t, :].rearrange("p (h d) -> p h d", h=HEADS),
                                  M[1 + b][:, i * BW:(i + 1) * BW].rearrange("p (h d) -> p h d", h=HEADS), d, ALU.mult)
                    last.then_inc(sem("xdt"), 1)

            def st_acs():
                dve.wait_ge(sem("acs_ps"), 1)
                v.tensor_copy(acs, M[3][:, 0:16]).then_inc(sem("acs"), 1)
                spread(0)

            def st_cb(g):
                dve.wait_ge(sem("cb_sb"), g + 1)
                for a, _ in REG:
                    last = tt(cbs[:, a:a + P], cbs[:, a:a + P], u_incl, ALU.mult)
                last.then_inc(sem("cbs"), 1)

            def st_mh1(h):
                dve.wait_ge(sem("acsb_ps"), h + 1)
                if h >= 1:
                    dve.wait_ge(sem("y_ps"), h)
                else:
                    dve.wait_ge(sem("acs"), 1)
                for n, (a, w) in enumerate(REG):
                    last = ts(dec[:, a:a + w], M[3][:, n * P:SEQ], acs[:, n * HEADS + h:n * HEADS + h + 1], 0.0,
                              ALU.subtract, ALU.min)
                last.then_inc(sem("seg"), 1)
                if h + 1 < HEADS:
                    spread(h + 1)
                dve.wait_ge(sem("decay"), h + 1)
                dve.wait_ge(sem("cbs"), h // 2 + 1)
                tt(dec[:, :], dec[:, :], cbs[:, :], ALU.mult).then_inc(sem("mt"), 1)

            def st_mh2(h):
                if h % 2 == 0:
                    return
                f = h // 2
                dve.wait_ge(sem("y_ps"), h + 1)
                link(stt(out=xs[:, f, :], in0=xs[:, f, :], scalar=pcol("dsk", f), in1=M[0][:, :], op0=ALU.mult, op1=ALU.add))
                tt(sz[:, f, :], xs[:, f, :], sz[:, f, :], ALU.mult).then_inc(sem("y_mid"), 1)

            def st_mn(g):
                dve.wait_ge(sem("yrstd"), g + 1)
                stt(out=sz[:, g, :], in0=sz[:, g, :], scalar=pcol("ng", g), in1=mrs[:, g, :], op0=ALU.mult, op1=ALU.mult)\
                    .then_inc(sem("yn"), 1)
                dve.wait_ge(sem("yc_hi"), g + 1)
                tt(yl[1][:, g, :], sz[:, g, :], as_f32(yh[1][:, g, :]), ALU.subtract).then_inc(sem("yc_lo"), 1)

            def st_mo1(h):
                dve.wait_ge(sem("mo_s"), h + 1)
                for c in range(TT):
                    b, o = QBANK[c]
                    diag = M[b][:, o + c * P:o + (c + 1) * P]
                    last = tt(diag, diag, negmask, ALU.add)
                link(last)
                for c in range(TT):
                    b, o = QBANK[c]
                    last = v.reduce_max(mmx[:, c:c + 1], M[b][:, o:o + (c + 1) * P], AX.X)
                link(last)
                if h >= 1:
                    dve.wait_ge(sem("mo_e"), h)
                ts(mnm, mmx, -1.0, None, ALU.mult).then_inc(sem("mo_nm"), 1)
                dve.wait_ge(sem("mo_e"), h + 1)
                link(v.reciprocal(mrl, mls))
                for c in range(TT):
                    a, w = QREG[c]
                    last = ts(mp[:, a:a + w], mp[:, a:a + w], mrl[:, c:c + 1], None, ALU.mult)
                last.then_inc(sem("mo_p"), 1)

            def out_lo(hi_name, dst_h, dst_l, name, h):
                if h % 2:
                    f = h // 2
                    dve.wait_ge(sem(hi_name), f + 1)
                    tt(dst_l[:, f, :], M[3][:, :], as_f32(dst_h[:, f, :]), ALU.subtract).then_inc(sem(name), 1)

            def st_mo3(h):
                out_lo("yd_hi", ydh, ydl, "yd_lo", h)

            def st_st1(h):
                dve.wait_ge(sem("st_ln"), h + 1)
                for b, c, a, w in RUNS:
                    last = stt(out=stsp[:, a:a + w], in0=M[b][:, c:c + w], scalar=0.0, in1=stl[:, a:a + w], op0=ALU.max, op1=ALU.add)
                link(last)
                for a, _ in REG:
                    last = tt(stsp[:, a:a + P], stsp[:, a:a + P], u_strict, ALU.mult)
                last.then_inc(sem("st_sp"), 1)
                for b, c, a, w in RUNS:
                    stt(out=stl[:, a:a + w], in0=M[b][:, c:c + w], scalar=0.0, in1=stl[:, a:a + w], op0=ALU.min, op1=ALU.subtract)
                dve.wait_ge(sem("st_hi"), h + 1)
                tt(st_l[:, :], stsp[:, :], as_f32(st_h[:, :]), ALU.subtract).then_inc(sem("st_lo"), 1)

            def st_st2(h):
                dve.wait_ge(sem("st_b"), h + 1)
                dve.wait_ge(sem("st_lo"), h + 1)
                for b, c, a, w in RUNS:
                    last = tt(stl[:, a:a + w], stl[:, a:a + w], M[b][:, c:c + w], ALU.subtract)
                last.then_inc(sem("st_arg"), 1)
                dve.wait_ge(sem("st_we"), h + 1)
                for a, _ in REG:
                    last = tt(stl[:, a:a + P], stl[:, a:a + P], u_strict, ALU.mult)
                last.then_inc(sem("st_w"), 1)

            def st_st3(h):
                out_lo("yb_hi", yh[0], yl[0], "yb_lo", h)

            none = lambda *a: None
            stages = {"dt": st_dt, "dtT": st_dtT, "xsT": st_xsT, "acs": st_acs, "cb": st_cb, "mh1": st_mh1, "mh2": st_mh2, "mn": st_mn,
                      "mo1": st_mo1, "mo2": none, "mo3": st_mo3, "st1": st_st1, "st2": st_st2, "st3": st_st3}

            for n in range(N_A):
                for j in range(2):
                    T = tiles_before(n) + j
                    if n == 0:
                        scaled(T, xa[:, j, :])
                    elif n == 1:
                        scaled(T, bgate[:, j, :])
                    elif n == 2:
                        scaled(T, cbuf[:, j, 2:])
                        if j == 1:
                            for f in range(2):
                                conv_a(f)
                            for f in range(2):
                                dve.wait_ge(sem("ya_hi"), f + 1)
                                tt(yl[0][:, f, :], xa[:, f, :], as_f32(yh[0][:, f, :]), ALU.subtract).then_inc(sem("ya_lo"), 1)
                    elif n in (3, 4):
                        f = 2 * (n - 3) + j
                        scaled(T, xbuf[:, f, 3:])
                        conv_c(f)
                    elif n == 5:
                        scaled(T, sz[:, j, :], 0.5)
                    elif n in (6, 9):
                        scaled(T, (qd if n == 6 else qb)[:, j, :], DH ** -0.5)
                    elif n in (7, 10):
                        scaled(T, (kd if n == 7 else kb)[:, j, :])
                    else:
                        d = vd if n == 8 else vb
                        scaled_tm(T, [(2 * j + i, d[:, 2 * j + i, :]) for i in range(2)], BW)
                    i = 2 * n + j - 7
                    if 0 <= i < 6:
                        d = (conv_dst + [sz[:, 0, :], sz[:, 1, :]])[i]
                        silu_out(i, d, d)
                    run_mix(stages, 2 * n + j)

            for i in range(N_B):
                n, br = n_b0 + i, i // 4
                for j in range(2):
                    t, T = 2 * i + j, tiles_before(n_b0 + i) + 2 * j
                    m, g = t % KD, gt[:, t % 2, :]
                    tile_ready(T)
                    tt(g, G[T % 4][:, :], R[:, :], ALU.mult).then_inc(sem("tile_free"), 1)
                    dve.wait_ge(sem("gate"), t + 1)
                    tile_ready(T + 1)
                    if br == 0:
                        stt(out=merged[:, m, :], in0=g, scalar=1.0, in1=G[(T + 1) % 4][:, :], op0=ALU.add, op1=ALU.mult)\
                            .then_inc(sem("tile_free"), 1)
                    else:
                        stt(out=g, in0=g, scalar=1.0, in1=G[(T + 1) % 4][:, :], op0=ALU.add, op1=ALU.mult)\
                            .then_inc(sem("tile_free"), 1)
                        dve.wait_ge(sem("tile_free"), T + 2)
                        last = tt(merged[:, m, :], merged[:, m, :], g, ALU.add)
                        if br == 3:
                            last.then_inc(sem("m_sum"), 1)
                            for mm_ in ([m - 1] if m else []) + ([m] if m == KD - 1 else []):
                                dve.wait_ge(sem("m_hi"), mm_ + 1)
                                stt(out=ml[:, mm_, :], in0=merged[:, mm_, :], scalar=0.5, in1=as_f32(mh[:, mm_, :]),
                                    op0=ALU.mult, op1=ALU.subtract).then_inc(sem("m_lo"), 1)
                        else:
                            link(last)
                    run_mix(stages, 24 + t)

            def accumulate(acc, sq, m, name):
                if m == 0:
                    v.tensor_copy(acc[:, :], sq[:, 0, :]).then_inc(sem(name), 1)
                else:
                    dve.wait_ge(sem(name), m)
                    tt(acc[:, :], acc[:, :], sq[:, m % 2, :], ALU.add).then_inc(sem(name), 1)

            def add_residual(T, m):
                tile_ready(T)
                tt(xT[:, m, :], xT[:, m, :], G[T % 4][:, :], ALU.add).then_inc(sem("tile_free"), 1)

            for m in range(KD):
                add_residual(tiles_before(n_c0) + m, m)
                dve.wait_ge(sem("sq0"), m + 1)
                accumulate(acc0, sq0, m, "acc0")
                dve.wait_ge(sem("h2_hi"), m + 1)
                stt(out=hl[:, m, :], in0=xT[:, m, :], scalar=pcol("g2", m), in1=as_f32(hh[:, m, :]),
                    op0=ALU.mult, op1=ALU.subtract).then_inc(sem("h2_lo"), 1)
            dve.wait_ge(sem("R2"), 1)

            def hidden_pair(i, n0, h0, before):
                for j in range(2):
                    T, s = tiles_before(n0 + j), (n0 + j) % 2
                    u = bass.ds(2 * i + j, 1)
                    flat = lambda t: t[:, u, :].rearrange("p a s -> p (a s)")
                    dve.wait_ge(sem("tile_done"), 4 * i + T + 1)
                    tt(fg_t[:, s, :], G[T % 4][:, :], R[:, :], ALU.mult).then_inc(sem("tile_free"), 1)
                    dve.wait_ge(sem("tile_done"), 4 * i + T + 2)
                    tt(fu_t[:, s, :], G[(T + 1) % 4][:, :], R[:, :], ALU.mult).then_inc(sem("tile_free"), 1)
                    dve.wait_ge(sem("tile_free"), 4 * i + T + 2)
                    dve.wait_ge(sem("gate_act"), 2 * i + h0 + j + 1)
                    tt(fu_t[:, s, :], fu_t[:, s, :], fg_t[:, s, :], ALU.mult).then_inc(sem("dve_link"), 1)
                    dve.wait_ge(sem("dve_link"), 4 * i + before + 2 * j + 1)
                    ts(flat(ah), fu_t[:, s, :], 1.0, None, ALU.mult).then_inc(sem("dve_link"), 1)
                    dve.wait_ge(sem("dve_link"), 4 * i + before + 2 * j + 2)
                    tt(flat(al), fu_t[:, s, :], as_f32(flat(ah)), ALU.subtract).then_inc(sem("act_lo"), 1)

            for f, (n0, part, h0) in enumerate(ffn_units):
                with dve.Fori(0, part // 2) as i:
                    hidden_pair(i, n0, h0, links[0])
                links[0] += 2 * part
                T0 = tiles_before(n0 + part)
                if f < len(FFN_PARTS) - 1:
                    with dve.Fori(0, 2) as i:
                        for q in range(4):
                            tile = xT[:, bass.ds(4 * i + q, 1), :].rearrange("p a s -> p (a s)")
                            dve.wait_ge(sem("tile_done"), 4 * i + T0 + q + 1)
                            tt(tile, tile, G[(T0 + q) % 4][:, :], ALU.add).then_inc(sem("tile_free"), 1)
                    dve.wait_ge(sem("tile_free"), T0 + KD)
                    continue
                for m in range(KD):
                    add_residual(T0 + m, m)
                    dve.wait_ge(sem("sq12"), m + 1)
                    accumulate(acc1, sq1, m, "acc1")
                    accumulate(acc2, sq2, m, "acc2")
                    dve.wait_ge(sem("h3_hi"), m + 1)
                    stt(out=hl[:, m, :], in0=xT[:, m, :], scalar=fgng[:, m:m + 1], in1=as_f32(hh[:, m, :]),
                        op0=ALU.mult, op1=ALU.subtract).then_inc(sem("h3_lo"), 1)

            dve.wait_ge(sem("r1_sq"), 1)
            tt(r2[:, :], M[1][:, :], r2[:, :], ALU.mult).then_inc(sem("n3_var"), 1)
            dve.wait_ge(sem("r1"), 1)
            dve.wait_ge(sem("r2"), 1)
            tt(R[:, :], r1[:, :], r2[:, :], ALU.mult).then_inc(sem("R3"), 1)

            T = tiles_before(n_e0)
            dve.wait_ge(sem("c2_in"), 80)
            tile_ready(T)
            dve.wait_ge(sem("R3"), 1)
            tt(rope_q[:, 0, :], G[T % 4][:, :], R[:, :], ALU.mult).then_inc(sem("tile_free"), 1)
            tile_ready(T + 1)
            tt(rope_t[:, 1, :], G[(T + 1) % 4][:, :], R[:, :], ALU.mult).then_inc(sem("tile_free"), 1)
            for m in range(KD):
                last = stt(out=xT[:, m, :], in0=xT[:, m, :], scalar=pcol("fg", m), in1=r1[:, :], op0=ALU.mult, op1=ALU.mult)
            link(last)
            dve.wait_ge(sem("rcol_ps"), 1)
            v.tensor_copy(rcol, M[2][:, :].rearrange("p (t c) -> p t c", t=TT)[:, :, 0]).then_inc(sem("rcol_read"), 1)
            dve.wait_ge(sem("wT_ps"), 1)
            for b in range(2):
                last = v.tensor_copy(wT[:, 4 * b:4 * b + 4, :].rearrange("p g i -> p (g i)"), M[b][:, :])
            last.then_inc(sem("wT_read"), 1)
            dve.wait_ge(sem("wT_read"), 1)
            v.memset(wT[64:P, :, 0:64], 0.0).then_inc(sem("wT_ready"), 1)

            def rope(i, j, bank):
                dve.wait_ge(sem("rope_ps"), i + 1)
                tt(rope_t[:, j, :], bank[:, :], cs2[:, 1, :], ALU.mult)
                link(tt(rope_q[:, j, :], rope_q[:, j, :], cs2[:, 0, :], ALU.mult))

            def finish_keys():
                rope(0, 0, M[3])
                for kv in range(2):
                    for half in range(2):
                        r = slice(64 * kv, 64 * kv + 64)
                        last = tt(k2[64 * half:64 * half + 64, kv, :], rope_q[r, 0, :], rope_t[r, 0, :], ALU.add)
                dve.wait_ge(sem("v2_ps"), 1)
                last = v.tensor_copy(v2[:, :, :].rearrange("p t c -> p (t c)"), M[2][:, :])
                last.then_inc(sem("k_ready"), 1)
                dve.wait_ge(sem("k_ready"), 1)

            pos = [0]
            mask = perm[:, P:P + 256]

            def w_soft(s):
                m, c = s // TT, s % TT
                b, sl = 2 * (s % 3), s % 3
                c0 = P if c == 0 else 0
                dve.wait_ge(sem("w_ps"), s + 1)
                if s >= 3:
                    dve.wait_ge(sem("w_t"), s - 2)
                for h in range(2):
                    last = tt(wp[:, sl, h, c0:256], M[h][:, c0:256], mask[:, c0:256], ALU.add)
                last.then_inc(sem("w_s"), 1)
                dve.wait_ge(sem("w_s"), s + 1)
                link(v.reduce_max(wmx[:, b:b + 2], wp[:, sl, :, c0:256], AX.X))
                link(tt(wmx[:, b:b + 2], wmx[:, b:b + 2], pcol("sink", 2 * m, 2), ALU.max))
                link(ts(wnm[:, b:b + 2], wmx[:, b:b + 2], -1.0, None, ALU.mult))
                tt(wes[:, b:b + 2], wnm[:, b:b + 2], pcol("sink", 2 * m, 2), ALU.add).then_inc(sem("w_nm"), 1)

            def w_norm(s):
                b, sl = 2 * (s % 3), s % 3
                c0 = P if s % TT == 0 else 0
                dve.wait_ge(sem("w_e"), s + 1)
                link(tt(wls[:, b:b + 2], wls[:, b:b + 2], wes[:, b:b + 2], ALU.add))
                link(v.reciprocal(wls[:, b:b + 2], wls[:, b:b + 2]))
                for h in range(2):
                    last = ts(wp[:, sl, h, c0:256], wp[:, sl, h, c0:256], wls[:, b + h:b + h + 1], None, ALU.mult)
                last.then_inc(sem("w_p"), 1)

            def w_out(s):
                if s % TT == TT - 1:
                    m = s // TT
                    dve.wait_ge(sem("w_v"), s + 1)
                    tt(att_t[:, :], M[3][:, :], za_tile(m), ALU.mult).then_inc(sem("w_o"), 1)

            def w_rest(s):
                if s % TT == TT - 1:
                    m = s // TT
                    dve.wait_ge(sem("at_hi"), m + 1)
                    tt(atl[:, m, :], att_t[:, :], as_f32(ath[:, m, :]), ALU.subtract).then_inc(sem("at_lo"), 1)

            def w_slot(limit):
                i = pos[0]
                if i >= limit and limit < STEPS:
                    return
                if 0 <= i - 1 < STEPS:
                    w_norm(i - 1)
                if 0 <= i - 5 < STEPS:
                    w_rest(i - 5)
                if 0 <= i - 4 < STEPS:
                    w_out(i - 4)
                if i < STEPS:
                    w_soft(i)
                pos[0] += 1

            def gate_attention(p):
                for m in (2 * p, 2 * p + 1):
                    dve.wait_ge(sem("za_e"), m + 1)
                    stt(out=za_tile(m), in0=za_e[:, m % 2, :], scalar=1.0, in1=za_tile(m), op0=ALU.add, op1=ALU.mult)\
                        .then_inc(sem("za"), 1)
                dve.wait_ge(sem("za"), 2 * p + 2)

            for p in range(4):
                n = n_qz + 2 * p
                lim = W_PER * p
                for u in range(2):
                    for j in range(2):
                        m, T = 2 * p + j, tiles_before(n + u) + j
                        w_slot(lim)
                        if j == 0:
                            w_slot(lim)
                        if u == 1 and j == 0:
                            for i in range(2):
                                rope(1 + 2 * p + i, i, G[(tiles_before(n) + i) % 4])
                                tt(q2[:, (2 * p + i) % 4, :], rope_q[:, i, :], rope_t[:, i, :], ALU.add).then_inc(sem("tile_free"), 1)
                        tile_ready(T)
                        if u == 0:
                            if p == 0 and j == 0:
                                finish_keys()
                            stt(out=rope_q[:, j, :], in0=G[T % 4][:, :], scalar=DH ** -0.5, in1=R[:, :], op0=ALU.mult, op1=ALU.mult)\
                                .then_inc(sem("rope_in"), 1)
                        else:
                            scaled(T, za_tile(m), 0.5)
                        if p >= 1 and u == 0 and j == 1:
                            gate_attention(p - 1)
            for p in range(4):
                n = n_vs + p
                for j in range(2):
                    T = tiles_before(n) + j
                    w_slot(STEPS)
                    w_slot(STEPS)
                    tile_ready(T)
                    for i in range(2):
                        t = (T % 2) * 2 + i
                        last = ts(vg[:, t, p * UC:(p + 1) * UC], G[T % 4][:, i * UC:(i + 1) * UC], rcol[:, t:t + 1], None, ALU.mult)
                    last.then_inc(sem("tile_free"), 1)
                    dve.wait_ge(sem("tile_free"), T + 1)
                    if p == 0 and j == 1:
                        gate_attention(3)
            while pos[0] < STEPS + 5:
                w_slot(STEPS)

            def layer_norm_stats():
                for t in range(TT):
                    dve.wait_ge(sem("vs_act"), t + 1)
                    for half in range(2):
                        last = v.bn_stats(bns[:, (2 * t + half) * 6:(2 * t + half + 1) * 6], vg[:, t, half * 512:(half + 1) * 512])
                link(last)
                for t in range(TT):
                    last = v.bn_aggr(mv[:, 2 * t:2 * t + 2], bns[:, 12 * t:12 * t + 12])
                link(last)
                link(ts(lrs, mv.rearrange("p (t a) -> p t a", a=2)[:, :, 1], EPS, None, ALU.add))
                v.reciprocal(lrs, lrs).then_inc(sem("ln_var"), 1)
                dve.wait_ge(sem("ln_rs"), 1)

            def layer_norm(t):
                link(ts(vg[:, t, :], vg[:, t, :], mv[:, 2 * t:2 * t + 1], lrs[:, t:t + 1], ALU.subtract, ALU.mult))
                link(tt(vg[:, t, :], vg[:, t, :], lng[:, :], ALU.mult))
                tt(vg[:, t, :], vg[:, t, :], lnb[:, :], ALU.add).then_inc(sem("vb_ready"), 1)

            def gates(n0, buf, second):
                for p in range(4):
                    n = n0 + 2 * p
                    for j in range(2):
                        scaled(tiles_before(n) + j, buf[:, j, :])
                    if not second:
                        if p == 0:
                            layer_norm_stats()
                        layer_norm(p)
                    for j in range(2):
                        m, T = 2 * p + j, tiles_before(n + 1) + j
                        dve.wait_ge(sem("gm_act"), m + 1 + (KD if second else 0))
                        tile_ready(T)
                        if not second:
                            tt(y2[:, m, :], G[T % 4][:, :], buf[:, j, :], ALU.mult).then_inc(sem("tile_free"), 1)
                            dve.wait_ge(sem("tile_free"), T + 1)
                        else:
                            tt(buf[:, j, :], G[T % 4][:, :], buf[:, j, :], ALU.mult).then_inc(sem("tile_free"), 1)
                            dve.wait_ge(sem("tile_free"), T + 1)
                            tt(y2[:, m, :], y2[:, m, :], buf[:, j, :], ALU.add).then_inc(sem("y2_sum"), 1)
                            dve.wait_ge(sem("y2_hi"), m + 1)
                            tt(y2l[:, m, :], y2[:, m, :], as_f32(y2h[:, m, :]), ALU.subtract).then_inc(sem("y2_lo"), 1)

            gates(n_ga, g2t, False)
            for p in range(4):
                n = n_uz + 2 * p
                for j in range(2):
                    scaled(tiles_before(n) + j, ub[:, j, :])
                for j in range(2):
                    scaled(tiles_before(n + 1) + j, zb[:, j, :])
                for j in range(2):
                    m = 2 * p + j
                    dve.wait_ge(sem("mixed_ps"), m + 1)
                    d = sgt[:, j, :]
                    ins = tt(d.rearrange("p (t i) -> p t i", t=TT), M[m % 2][:, :].rearrange("p (t i) -> p t i", t=TT),
                             bsb[:, m, :].unsqueeze(1).broadcast_to((P, TT, P)), ALU.add)
                    ins.then_inc(sem("mixed"), 1)
                    dve.wait_ge(sem("mixed"), m + 1)
                    dve.wait_ge(sem("u_act"), m + 1)
                    link(tt(d, d, ub[:, j, :], ALU.mult))
                    dve.wait_ge(sem("zs_act"), m + 1)
                    tt(d, d, zb[:, j, :], ALU.mult).then_inc(sem("sg"), 1)
                    dve.wait_ge(sem("sg_hi"), m + 1)
                    tt(sgl[:, m, :], d, as_f32(sgh[:, m, :]), ALU.subtract).then_inc(sem("sg_lo"), 1)
            gates(n_gs, g4t, True)

            for m in range(KD):
                T = tiles_before(n_o2) + m
                add_residual(T, m)
                dve.wait_ge(sem("tile_free"), T + 1)
                if m >= 2:
                    dve.wait_ge(sem("o_ps"), m - 1)
                ts(fo[:, m % 2, :], xT[:, m, :], pcol("fg2", m), None, ALU.mult).then_inc(sem("fo"), 1)
                dve.wait_ge(sem("sq3"), m + 1)
                accumulate(acc3, sq3, m, "acc3")
            dve.wait_ge(sem("R4"), 1)
            dve.wait_ge(sem("o_copied"), KD)
            for t in (0, 2, 3):
                ts(ot[:, t, :], ot[:, t, :], rcol[:, t:t + 1], None, ALU.mult).then_inc(sem("out_dve"), 1)


def constants():
    i = np.arange(P)
    f = np.float32
    upper = np.concatenate([(i[:, None] <= i[None, :]).astype(f), np.ones((P, 3 * P), f)], 1)
    cst1 = np.concatenate([np.eye(P, dtype=f), upper, (i[:, None] < i[None, :]).astype(f),
                           (i[:, None] > i[None, :]).astype(f),
                           np.where(i[None, :] > i[:, None], f(NEG), f(0)).astype(f)], 1)
    half = 8
    inv = f(500000.0) ** (-(np.arange(half, dtype=f) * f(2.0)) / f(16))
    ang = np.arange(SEQ, dtype=f)[None, :] * inv[:, None].astype(f)
    cos, sin = np.ones((64, SEQ), f), np.zeros((64, SEQ), f)
    cos[0:8] = cos[8:16] = np.cos(ang)
    sin[0:8], sin[8:16] = -np.sin(ang), np.sin(ang)
    swap = np.zeros((P, P), f)
    for h in range(2):
        for d in range(half):
            swap[64 * h + d + half, 64 * h + d] = swap[64 * h + d, 64 * h + d + half] = 1
    win = np.zeros((P, 256), f)
    win[0:64, 192:256] = NEG
    win[64:128, 0:64] = NEG
    cst2a = np.concatenate([np.tile(cos, (2, 1)), np.tile(sin, (2, 1))], 1)
    return cst1, cst2a, np.concatenate([swap, win], 1)


def kernel(x, norm1_g, w_in, conv_a_w, ssm_conv_w, ssm_conv_b, ssm_dt_bias, ssm_a_log, ssm_d, ssm_norm_g, w_branch,
           w_o, norm2_g, w_gate_up, w_down, final_g, norm_g_2, w_in_2, b_merge_2, att_sinks_2, sg_w_2, sg_b_2,
           sg_ln_g_2, sg_ln_b_2, w_att_out_2, w_sg_out_2, w_o_2, final_g_2):
    import concourse.bacc as bacc
    from concourse.bass_utils import run_bass_kernel_spmd

    col = lambda a: np.asarray(a).reshape(-1, P).T
    row = lambda a: np.broadcast_to(np.asarray(a).reshape(1, -1), (P, np.asarray(a).size))
    par = np.ascontiguousarray(np.concatenate([
        col(norm1_g), col(conv_a_w), col(ssm_conv_w), col(ssm_conv_b), col(ssm_norm_g),
        np.repeat(np.asarray(ssm_d).reshape(2, 2).T, 64, axis=0), col(norm2_g), col(final_g), col(norm_g_2), col(b_merge_2),
        col(final_g_2), row(att_sinks_2), row(ssm_dt_bias), row(ssm_a_log),
        np.full((P, 1), EPS, np.float32)], axis=1))
    cst1, cst2a, cst2b = constants()
    a = np.asarray
    arrays = {
        "x": a(x)[0], "par": par, "cst1": cst1, "cst2a": cst2a, "cst2b": cst2b, "w_in": a(w_in)[0], "w_branch": a(w_branch)[0],
        "w_o": a(w_o)[0], "w_gu": a(w_gate_up)[0], "w_down": a(w_down)[0], "w_in2": a(w_in_2)[0], "sg_w": a(sg_w_2)[0],
        "sg_b": a(sg_b_2).reshape(-1), "ln_g": a(sg_ln_g_2).reshape(-1), "ln_b": a(sg_ln_b_2).reshape(-1),
        "w_ao": a(w_att_out_2)[0], "w_so": a(w_sg_out_2)[0], "w_o2": a(w_o_2)[0],
    }
    arrays = {k: np.ascontiguousarray(v) for k, v in arrays.items()}
    nc = bacc.Bacc("TRN2", target_bir_lowering=False, num_devices=1)
    ins = [nc.dram_tensor(k, v.shape, mybir.dt.from_np(v.dtype), kind="ExternalInput").ap() for k, v in arrays.items()]
    out = nc.dram_tensor("out", (SEQ, DM), mybir.dt.float32, kind="ExternalOutput").ap()
    build_program(nc, *ins, out)
    r = run_bass_kernel_spmd(nc, [arrays], core_ids=[0])
    return np.asarray(r.results[0]["out"]).reshape(1, SEQ, DM)
```
